# Optimizing a Trainium2 kernel written in Bass

```python
import math
import jax, jax.numpy as jnp
from jax import lax
import numpy as np

D_MODEL = 1024
BATCH = 1
SEQ = 512
DEPTH = 1

N_META = 16
EPS = 1e-6
GDN_HEADS = 8
GDN_DK = 64
GDN_DV = 64
CONV_K = 4
CHUNK = 64
GDN_QK_W = GDN_HEADS * GDN_DK
GDN_V_W = GDN_HEADS * GDN_DV
GDN_QKV_W = 2 * GDN_QK_W + GDN_V_W
MLA_HEADS = 8
Q_LORA = 256
KV_LORA = 128
QK_NOPE = 64
QK_ROPE = 32
QK_DIM = QK_NOPE + QK_ROPE
V_DIM = 64
ROPE_THETA = 10000.0
Q_BLOCK = 128
MIX_WIDTH = GDN_V_W + MLA_HEADS * V_DIM
IN_SPLITS = (GDN_QKV_W, GDN_V_W, GDN_HEADS, GDN_HEADS, Q_LORA, KV_LORA, QK_ROPE)
IN_WIDTH = sum(IN_SPLITS)
PEER_HEADS = 8
N_KEYS = 128
N_EXPERTS = N_KEYS * N_KEYS
PEER_QDIM = 256
PEER_HALF = PEER_QDIM // 2
PEER_TOPK = 16
PEER_BLOCK = 256

kernel_name = "hybrid_gdn_mla_peer_block"

def rms_norm(x, w):
    xf = x.astype(jnp.float32)
    y = xf * lax.rsqrt(jnp.mean(xf * xf, axis=-1, keepdims=True) + EPS)
    return (y * w.astype(jnp.float32)).astype(x.dtype)

def l2_norm(x):
    xf = x.astype(jnp.float32)
    return (xf * lax.rsqrt(jnp.sum(xf * xf, axis=-1, keepdims=True) + EPS)).astype(x.dtype)

def causal_depthwise_conv(x, w):
    K, C = w.shape
    return lax.conv_general_dilated(x, w[:, None, :].astype(x.dtype), window_strides=(1,), padding=[(K - 1, 0)], dimension_numbers=('NWC', 'WIO', 'NWC'), feature_group_count=C)

def apply_rope(x, pos):
    R = x.shape[-1]
    half = R // 2
    inv = jnp.exp(-math.log(ROPE_THETA) * jnp.arange(half, dtype=jnp.float32) * (2.0 / R))
    ang = pos.astype(jnp.float32)[:, None] * inv[None, :]
    cos = jnp.cos(ang)[:, None, :]
    sin = jnp.sin(ang)[:, None, :]
    xf = x.astype(jnp.float32)
    x1, x2 = xf[..., :half], xf[..., half:]
    return jnp.concatenate([x1 * cos - x2 * sin, x2 * cos + x1 * sin], axis=-1).astype(x.dtype)

def gated_delta_chunked(q, k, v, g, beta):
    out_dtype = v.dtype
    B, T, H, dk = q.shape
    n = T // CHUNK
    f32 = jnp.float32

    def to_chunks(t):
        return t.astype(f32).reshape(B, n, CHUNK, H, -1).transpose(1, 0, 3, 2, 4)

    q = to_chunks(q) * (dk ** -0.5)
    k = to_chunks(k)
    v = to_chunks(v)
    g = g.astype(f32).reshape(B, n, CHUNK, H).transpose(1, 0, 3, 2)
    beta = beta.astype(f32).reshape(B, n, CHUNK, H).transpose(1, 0, 3, 2)
    gc = jnp.cumsum(g, axis=-1)
    tril = jnp.tril(jnp.ones((CHUNK, CHUNK), dtype=bool))
    strict = jnp.tril(jnp.ones((CHUNK, CHUNK), dtype=bool), k=-1)
    decay = jnp.exp(jnp.where(tril, gc[..., :, None] - gc[..., None, :], -jnp.inf))
    kb = k * beta[..., None]
    vb = v * beta[..., None]
    m = jnp.where(strict, jnp.einsum('nbhid,nbhjd->nbhij', kb, k) * decay, 0.0)
    a_mat = m + jnp.eye(CHUNK, dtype=f32)
    rhs = jnp.concatenate([vb, kb * jnp.exp(gc)[..., None]], axis=-1)
    sol = lax.linalg.triangular_solve(a_mat, rhs, left_side=True, lower=True, unit_diagonal=True)
    u = sol[..., :v.shape[-1]]
    w = sol[..., v.shape[-1]:]
    qk = jnp.einsum('nbhid,nbhjd->nbhij', q, k) * decay
    qg = q * jnp.exp(gc)[..., None]
    kd = k * jnp.exp(gc[..., -1:] - gc)[..., None]
    gl = jnp.exp(gc[..., -1])

    def step(S, inp):
        qk_c, qg_c, u_c, w_c, kd_c, gl_c = inp
        v_new = u_c - jnp.einsum('bhcd,bhde->bhce', w_c, S)
        o = jnp.einsum('bhcd,bhde->bhce', qg_c, S) + jnp.einsum('bhij,bhje->bhie', qk_c, v_new)
        S = S * gl_c[..., None, None] + jnp.einsum('bhcd,bhce->bhde', kd_c, v_new)
        return S, o

    S0 = jnp.zeros((B, H, dk, v.shape[-1]), f32)
    _, o = lax.scan(step, S0, (qk, qg, u, w, kd, gl))
    return o.transpose(1, 0, 3, 2, 4).reshape(B, T, H, -1).astype(out_dtype)

def gdn_mixer(qkv_raw, z, b, a, conv_w, a_log, dt_bias, gdn_norm):
    B, L, _ = qkv_raw.shape
    qkv = jax.nn.silu(causal_depthwise_conv(qkv_raw, conv_w))
    q, k, v = jnp.split(qkv, [GDN_QK_W, 2 * GDN_QK_W], axis=-1)
    q = l2_norm(q.reshape(B, L, GDN_HEADS, GDN_DK))
    k = l2_norm(k.reshape(B, L, GDN_HEADS, GDN_DK))
    v = v.reshape(B, L, GDN_HEADS, GDN_DV)
    beta = jax.nn.sigmoid(b.astype(jnp.float32))
    g = -jnp.exp(a_log.astype(jnp.float32)) * jax.nn.softplus(a.astype(jnp.float32) + dt_bias.astype(jnp.float32))
    pad = (-N_META) % CHUNK

    def lpad(t):
        return jnp.pad(t, ((0, 0), (pad, 0)) + ((0, 0),) * (t.ndim - 2))

    o = gated_delta_chunked(lpad(q), lpad(k), lpad(v), lpad(g), lpad(beta))[:, pad:]
    o = rms_norm(o, gdn_norm) * jax.nn.silu(z.reshape(B, L, GDN_HEADS, GDN_DV))
    return o.reshape(B, L, GDN_V_W)

def blocked_causal_attention(q, k, v):
    B, L, H, dq = q.shape
    Lp = -(-L // Q_BLOCK) * Q_BLOCK

    def rpad(t):
        return jnp.pad(t, ((0, 0), (0, Lp - L), (0, 0), (0, 0)))

    q, k, v = rpad(q), rpad(k), rpad(v)
    scale = dq ** -0.5
    kpos = jnp.arange(Lp)

    def block(i):
        start = i * Q_BLOCK
        qb = lax.dynamic_slice_in_dim(q, start, Q_BLOCK, axis=1)
        s = jnp.einsum('bqhd,bkhd->bhqk', qb, k).astype(jnp.float32) * scale
        qpos = start + jnp.arange(Q_BLOCK)
        s = jnp.where(kpos[None, :] <= qpos[:, None], s, -jnp.inf)
        p = jax.nn.softmax(s, axis=-1).astype(v.dtype)
        return jnp.einsum('bhqk,bkhd->bqhd', p, v)

    o = lax.map(block, jnp.arange(Lp // Q_BLOCK))
    return o.transpose(1, 0, 2, 3, 4).reshape(B, Lp, H, -1)[:, :L]

def mla_mixer(cq, ckv, kpe, q_a_norm, kv_a_norm, w_uq, w_ukv, q_norm, k_norm, pos):
    B, L, _ = cq.shape
    qh = (rms_norm(cq, q_a_norm) @ w_uq).reshape(B, L, MLA_HEADS, QK_DIM)
    kv = (rms_norm(ckv, kv_a_norm) @ w_ukv).reshape(B, L, MLA_HEADS, QK_NOPE + V_DIM)
    k_nope, v = kv[..., :QK_NOPE], kv[..., QK_NOPE:]
    k_pe = jnp.broadcast_to(kpe[:, :, None, :], (B, L, MLA_HEADS, QK_ROPE))
    kh = jnp.concatenate([k_nope, k_pe], axis=-1)
    qh = rms_norm(qh, q_norm)
    kh = rms_norm(kh, k_norm)
    qh = jnp.concatenate([qh[..., :QK_NOPE], apply_rope(qh[..., QK_NOPE:], pos)], axis=-1)
    kh = jnp.concatenate([kh[..., :QK_NOPE], apply_rope(kh[..., QK_NOPE:], pos)], axis=-1)
    o = blocked_causal_attention(qh, kh, v)
    return o.reshape(B, L, MLA_HEADS * V_DIM)

def peer(xn, w_pq, sub_keys, expert_u, expert_v):
    B, L, D = xn.shape
    q = (xn @ w_pq).reshape(B, L, PEER_HEADS, 2, PEER_HALF).astype(jnp.float32)
    s = jnp.einsum('blhpc,hpkc->blhpk', q, sub_keys.astype(jnp.float32))
    sv, si = lax.top_k(s, PEER_TOPK)
    cand = (sv[..., 0, :, None] + sv[..., 1, None, :]).reshape(B, L, PEER_HEADS, PEER_TOPK * PEER_TOPK)
    cv, ci = lax.top_k(cand, PEER_TOPK)
    i1 = jnp.take_along_axis(si[..., 0, :], ci // PEER_TOPK, axis=-1)
    i2 = jnp.take_along_axis(si[..., 1, :], ci % PEER_TOPK, axis=-1)
    experts = i1 * N_KEYS + i2
    gates = jax.nn.softmax(cv, axis=-1)
    T = B * L
    E = PEER_HEADS * PEER_TOPK
    Tp = -(-T // PEER_BLOCK) * PEER_BLOCK
    nb = Tp // PEER_BLOCK
    x_flat = jnp.pad(xn.reshape(T, D), ((0, Tp - T), (0, 0))).reshape(nb, PEER_BLOCK, D)
    e_flat = jnp.pad(experts.reshape(T, E), ((0, Tp - T), (0, 0))).reshape(nb, PEER_BLOCK, E)
    g_flat = jnp.pad(gates.reshape(T, E).astype(xn.dtype), ((0, Tp - T), (0, 0))).reshape(nb, PEER_BLOCK, E)

    def block(args):
        xb, eb, gb = args
        h = jnp.einsum('ped,pd->pe', expert_u[eb], xb)
        return jnp.einsum('pe,ped->pd', jax.nn.gelu(h, approximate=False) * gb, expert_v[eb])

    y = lax.map(block, (x_flat, e_flat, g_flat))
    return y.reshape(Tp, D)[:T].reshape(B, L, D)

def setup_inputs(seed: int = 0) -> dict:
    key = jax.random.key(seed)
    ks = jax.random.split(key, 24)
    f32 = jnp.float32

    def nrm(k, shape, s):
        return jax.random.normal(k, shape, f32) * s

    def gain(k, shape):
        return 1.0 + 0.02 * jax.random.normal(k, shape, f32)

    dt = jnp.exp(jax.random.uniform(ks[6], (DEPTH, GDN_HEADS), f32, math.log(1e-3), math.log(1e-1)))
    return {
        'x': nrm(ks[0], (BATCH, SEQ, D_MODEL), 1.0),
        'meta_tokens': nrm(ks[1], (N_META, D_MODEL), 1.0),
        'attn_norm': gain(ks[2], (DEPTH, D_MODEL)),
        'w_in': nrm(ks[3], (DEPTH, D_MODEL, IN_WIDTH), D_MODEL ** -0.5),
        'conv_w': nrm(ks[4], (DEPTH, CONV_K, GDN_QKV_W), 0.5),
        'a_log': jnp.log(jax.random.uniform(ks[5], (DEPTH, GDN_HEADS), f32, 1.0, 16.0)),
        'dt_bias': dt + jnp.log(-jnp.expm1(-dt)),
        'gdn_norm': gain(ks[7], (DEPTH, GDN_DV)),
        'q_a_norm': gain(ks[8], (DEPTH, Q_LORA)),
        'kv_a_norm': gain(ks[9], (DEPTH, KV_LORA)),
        'w_uq': nrm(ks[10], (DEPTH, Q_LORA, MLA_HEADS * QK_DIM), Q_LORA ** -0.5),
        'w_ukv': nrm(ks[11], (DEPTH, KV_LORA, MLA_HEADS * (QK_NOPE + V_DIM)), KV_LORA ** -0.5),
        'q_norm': gain(ks[12], (DEPTH, QK_DIM)),
        'k_norm': gain(ks[13], (DEPTH, QK_DIM)),
        'w_out': nrm(ks[14], (DEPTH, MIX_WIDTH, D_MODEL), MIX_WIDTH ** -0.5),
        'ffn_norm': gain(ks[15], (DEPTH, D_MODEL)),
        'w_pq': nrm(ks[16], (DEPTH, D_MODEL, PEER_HEADS * PEER_QDIM), D_MODEL ** -0.5),
        'sub_keys': nrm(ks[17], (DEPTH, PEER_HEADS, 2, N_KEYS, PEER_HALF), PEER_HALF ** -0.5),
        'expert_u': nrm(ks[18], (DEPTH, N_EXPERTS, D_MODEL), D_MODEL ** -0.5),
        'expert_v': nrm(ks[19], (DEPTH, N_EXPERTS, D_MODEL), 0.5),
    }

def reference(x, meta_tokens, attn_norm, w_in, conv_w, a_log, dt_bias, gdn_norm, q_a_norm, kv_a_norm, w_uq, w_ukv, q_norm, k_norm, w_out, ffn_norm, w_pq, sub_keys, expert_u, expert_v):
    B = x.shape[0]
    meta = jnp.broadcast_to(meta_tokens[None].astype(x.dtype), (B, N_META, D_MODEL))
    h = jnp.concatenate([meta, x], axis=1)
    L = h.shape[1]
    pos = jnp.arange(L, dtype=jnp.int32)
    split_at = np.cumsum(IN_SPLITS)[:-1]
    for l in range(DEPTH):
        hn = rms_norm(h, attn_norm[l])
        proj = hn @ w_in[l]
        qkv_raw, z, b, a, cq, ckv, kpe = jnp.split(proj, split_at, axis=-1)
        y_gdn = gdn_mixer(qkv_raw, z, b, a, conv_w[l], a_log[l], dt_bias[l], gdn_norm[l])
        y_mla = mla_mixer(cq, ckv, kpe, q_a_norm[l], kv_a_norm[l], w_uq[l], w_ukv[l], q_norm[l], k_norm[l], pos)
        h = h + jnp.concatenate([y_gdn, y_mla], axis=-1) @ w_out[l]
        h = h + peer(rms_norm(h, ffn_norm[l]), w_pq[l], sub_keys[l], expert_u[l], expert_v[l])
    return h[:, N_META:]


_drawn_inputs = setup_inputs


def setup_inputs(seed=0):
    import zlib

    import numpy as np

    out = dict(_drawn_inputs(seed))
    spreads = {}
    factors = {'q_a_norm': 5.344,
     'kv_a_norm': 4.081,
     'q_norm': 5.043,
     'k_norm': 5.057,
     'gdn_norm': 8.0,
     'ffn_norm': 4.318}
    for name, (base, spread) in spreads.items():
        noise = np.random.default_rng([zlib.crc32(name.encode()), seed]).standard_normal(out[name].shape)
        drawn = base * np.exp(spread * noise) if base else spread * noise
        out[name] = __import__('jax').numpy.asarray(drawn.astype(out[name].dtype))
    for name, factor in factors.items():
        out[name] = (out[name] * factor).astype(out[name].dtype)
    return out
```

```python
from contextlib import ExitStack

import numpy as np

import concourse.bass as bass
from concourse import mybir

F32 = mybir.dt.float32
I32 = mybir.dt.int32
U32 = mybir.dt.uint32
ALU = mybir.AluOpType
ACT = mybir.ActivationFunctionType
AX = mybir.AxisListType.X

P = 128
D = 1024
SEQ = 512
META = 16
T = META + SEQ
KD = D // P
EPS = 1e-6
NEG = -1e30
H = 8
DK = 64
CONV = 4
QKV = 3 * H * DK
QC = QKV // P
REST = 944
Z0, B0, A0, CQ0, CKV0, KPE0 = 0, 512, 520, 528, 784, 912
QL, KL, NOPE, ROPE, QKD = 256, 128, 64, 32, 96
SCALE = QKD ** -0.5
LEVELS = 7
TOPK = 16
KEYS = 128
SLOTS = H * TOPK
XT = SEQ // P
SIZE = [META] + [P] * XT
START = [0] + [META + P * t for t in range(XT)]
NT = len(SIZE)
PARTS = [[0, 1, 2], [3, 4]]
WCOLS = 256
URING, DRING, RING, PAIR = 4, 4, 8, 2
BIG, BIGHALF = 8, 4


def chain(eng, sem):
    def link(ins):
        link.count += 1
        ins.then_inc(sem, 1)
        eng.wait_ge(sem, link.count)
    link.count = 0
    return link


class Tools:
    taken = {}

    def __init__(self, nc, ctx):
        self.nc, self.ctx, self.sems = nc, ctx, []
        ctx.callback(self.close)

    def close(self):
        if self.sems:
            self.nc.clear_and_free_semaphores(self.sems)
            self.nc.all_engine_barrier()

    def unique(self, name):
        n = self.taken[self.nc, name] = self.taken.get((self.nc, name), 0) + 1
        return name if n == 1 else f"{name}_{n}"

    def sb(self, name, shape, dt=F32):
        return self.ctx.enter_context(self.nc.sbuf_tensor(self.unique(name), shape, dt))

    def ps(self, name, shape, dt=F32):
        return self.ctx.enter_context(self.nc.psum_tensor(self.unique(name), shape, dt))

    def sem(self, name):
        self.sems.append(self.nc.alloc_semaphore(name=self.unique(name)))
        return self.sems[-1]


class Weights:
    def __init__(self, t, dram):
        self.buf = t.sb("w_blocks", [P, 2, KD, WCOLS])
        self.full = [t.sem("w_full0"), t.sem("w_full1")]
        self.plan = []
        for _ in PARTS:
            for name, width in (("w_in", QKV + REST), ("w_out", D), ("w_pq", 2 * H * P)):
                w = dram[name].rearrange("(k p) n -> p k n", p=P)
                self.plan += [w[:, :, a:min(a + WCOLS, width)] for a in range(0, width, WCOLS)]
        self.loaded = self.loaded_by_phase = self.taken = 0

    def load(self, sp, ends):
        first, last = self.loaded_by_phase, self.loaded_by_phase + len(ends)
        while self.loaded < min(last + 2, len(self.plan)):
            n, src = self.loaded, self.plan[self.loaded]
            if n - 2 >= first:
                sp.wait_ge(*ends[n - 2 - first])
            sp.dma_start(self.buf[:, n % 2, :, 0:src.shape[2]], src).then_inc(self.full[n % 2], 16)
            self.loaded += 1
        self.loaded_by_phase = last

    def take(self, pe):
        n = self.taken
        self.taken += 1
        pe.wait_ge(self.full[n % 2], 16 * (n // 2 + 1))
        return self.buf[:, n % 2, :, :]


class Mixing:
    def __init__(self, nc, whole, t, dram, cst, xn, h1, idx, gates, acc, out):
        self.ident, self.xn, self.h1, self.idx, self.gates = cst["ident"], xn, h1, idx, gates
        self.acc, self.out, self.u, self.v = acc, out, dram["expert_u"], dram["expert_v"]
        self.uring, self.vring = t.sb("uring", [P, URING, D]), t.sb("vring", [P, RING, D])
        self.dots, self.acts = t.sb("dots", [P, RING]), t.sb("acts", [P, RING])
        self.weights, self.diag = t.sb("weights", [P, RING]), t.sb("diag", [P, DRING, P])
        self.u_full = [whole.sem(f"u_full{i}") for i in range(URING)]
        self.v_full = [whole.sem(f"v_full{i}") for i in range(RING)]
        self.dotted, self.gelued, self.scaled = whole.sem("dotted"), whole.sem("gelued"), whole.sem("scaled")
        self.diag_s, self.combined = whole.sem("diag_s"), whole.sem("combined")
        self.seeded, self.rows_out, self.stored = whole.sem("seeded"), whole.sem("rows_out"), whole.sem("stored")
        self.at = {"pool": 0, "dve": 0, "act": 0, "pe": 0}

    def _next(self, engine, n):
        a = self.at[engine]
        self.at[engine] = a + n
        return range(a, a + n)

    def pool(self, pool, n):
        for i in self._next("pool", n):
            k, ku = i % RING, i % URING
            row = bass.IndirectOffsetOnAxis(ap=self.idx[:, i:i + 1].bitcast(U32), axis=0)
            if i >= URING:
                pool.wait_ge(self.dotted, i - URING + 1)
            pool.indirect_dma_start(self.uring[:, ku, :], None, self.u, row).then_inc(self.u_full[ku], 16)
            if i >= RING:
                pool.wait_ge(self.combined, i - RING + 1)
            pool.indirect_dma_start(self.vring[:, k, :], None, self.v, row).then_inc(self.v_full[k], 16)

    def dve(self, dve, n):
        for i in self._next("dve", n):
            k, ku, tt = i % RING, i % URING, i // SLOTS
            if i and i % SLOTS == 0:
                self.finish_tile(dve, tt - 1)
            dve.wait_ge(self.u_full[ku], 16 * (i // URING + 1))
            if i >= RING:
                dve.wait_ge(self.gelued, (i - RING) // PAIR + 1)
            dve.tensor_tensor_reduce(out=self.uring[:, ku, :], in0=self.uring[:, ku, :], in1=self.xn[:, tt, :],
                                     scale=1.0, scalar=0.0, op0=ALU.mult, op1=ALU.add,
                                     accum_out=self.dots[:, k:k + 1]).then_inc(self.dotted, 1)

    def finish_tile(self, dve, tt):
        dve.wait_ge(self.combined, SLOTS * (tt + 1))
        dve.tensor_copy(self.h1[:, tt, :], self.acc[:]).then_inc(self.rows_out, 1)

    def act(self, act, n):
        assert n % PAIR == 0
        for i in self._next("act", n)[::PAIR]:
            b, bd = i % RING, i % DRING
            act.wait_ge(self.dotted, i + PAIR)
            if i >= DRING:
                act.wait_ge(self.combined, i - DRING + PAIR)
            act.activation(self.acts[:, b:b + PAIR], self.dots[:, b:b + PAIR], ACT.Gelu).then_inc(self.gelued, 1)
            act.wait_ge(self.gelued, i // PAIR + 1)
            for m in range(PAIR):
                act.activation(self.weights[:, b + m:b + m + 1], self.acts[:, b + m:b + m + 1], ACT.Copy,
                               scale=self.gates[:, i + m:i + m + 1]).then_inc(self.scaled, 1)
            act.wait_ge(self.scaled, i + PAIR)
            for m in range(PAIR):
                act.activation(self.diag[:, bd + m, :], self.ident[:], ACT.Copy,
                               scale=self.weights[:, b + m:b + m + 1]).then_inc(self.diag_s, 1)

    def pe(self, pe, n):
        for i in self._next("pe", n):
            k, tt = i % RING, i // SLOTS
            if i % SLOTS == 0:
                self.seed(pe, tt)
            pe.wait_ge(self.v_full[k], 16 * (i // RING + 1))
            pe.wait_ge(self.diag_s, i + 1)
            for a in range(2):
                mm = pe.matmul(self.acc[:, a * 512:(a + 1) * 512], self.diag[:, i % DRING, :],
                               self.vring[:, k, a * 512:(a + 1) * 512], start=False, stop=False, skip_group_check=True)
            mm.then_inc(self.combined, 1)

    def seed(self, pe, tt):
        if tt:
            pe.wait_ge(self.rows_out, tt)
        for a in range(2):
            mm = pe.matmul(self.acc[:, a * 512:(a + 1) * 512], self.ident[:], self.h1[:, tt, a * 512:(a + 1) * 512],
                           start=True, stop=False, skip_group_check=True)


def rows(ap, n):
    return bass.AP(tensor=ap.tensor, offset=ap.offset, ap=[[0, n]] + [list(x) for x in ap.ap])
SHARE = {"project": 30, "delta_rule": 52, "attention": 34, "out_project": 14, "key_scores": 24,
         "choose_own": 8, "choose_first": 26, "choose_second": 26}


def project(nc, dram, cst, keep, W, mix, part, beats):
    with ExitStack() as ctx:
        t = Tools(nc, ctx)
        act_beats, pe_beats = later(beats, 1), later(beats, 2)
        tiles = PARTS[part]
        NJ, t0 = len(tiles), START[tiles[0]]
        TP = sum(SIZE[j] for j in tiles)
        hx, hs = t.sb("hx", [P, 2, D]), t.sb("hs", [P, 2, D])
        arow = t.sb("attn_norm_row", [P, D])
        hnT = t.sb("hnT", [P, KD, TP])
        raw = t.sb("raw", [P, 2, CONV - 1 + TP])
        ss, rs = t.sb("ss", [P, NJ]), t.sb("rs", [P, NJ])
        cw4 = t.sb("conv_rows", [CONV, QKV]) if part == 0 else None
        tp, pp = t.ps("turn_banks", [P, 2, 512]), t.ps("project_banks", [P, 4, 512])
        names = ("x_in0", "x_in1", "row_in", "cw_in", "squared", "rooted", "normed", "turned", "hnT_s", "cw_mm", "cw_s",
                 "hist_s", "proj", "pad_s", "raw_s", "tail_s", "conved", "silued", "rest_mm", "rest_s", "dch", "init")
        s = {n: t.sem("a_" + n) for n in names}
        ident, sT, rest, hist, cw = cst["ident"], keep["sT"], keep["rest"], keep["hist"], keep["cw"]
        NB = (REST + WCOLS - 1) // WCOLS
        jobs = [(a, jj) for a in range(NB) for jj in range(NJ) if tiles[jj] or a * WCOLS >= B0]
        block = ctx.enter_context(nc.Block())

        @block.sync
        def _(sp):
            if part == 0:
                for name in ("ident", "triu", "maskT", "mask", "levels", "pair_ones", "cos", "sin", "iota16"):
                    sp.dma_start(cst[name][:], dram["c_" + name]).then_inc(cst["loaded"], 16)
            sp.dma_start(arow[:], rows(dram["attn_norm"], P)).then_inc(s["row_in"], 16)
            for jj, j in enumerate(tiles):
                if jj >= 2:
                    sp.wait_ge(s["normed"], jj - 1)
                src = dram["meta"] if j == 0 else dram["x"][(j - 1) * P:j * P, :]
                sp.dma_start(hx[0:SIZE[j], jj % 2, :], src).then_inc(s[f"x_in{jj % 2}"], 16)
            if part == 0:
                sp.dma_start(cw4[:], dram["conv_w"]).then_inc(s["cw_in"], 16)
            ends = [(s["proj"], c + 2) for c in range(0, QC, 2)]
            ends += [(s["rest_mm"], sum(1 for b, _ in jobs if b <= a)) for a in range(NB)]
            W.load(sp, ends)

        @block.gpsimd
        def _(pool):
            mix.pool(pool, sum(beats.values()))

        @block.scalar
        def _(act):
            for jj, j in enumerate(tiles):
                n = SIZE[j]
                act.wait_ge(s[f"x_in{jj % 2}"], 16 * (jj // 2 + 1))
                if jj >= 2:
                    act.wait_ge(s["turned"], 2 * (jj - 1))
                act.activation(hs[0:n, jj % 2, :], hx[0:n, jj % 2, :], ACT.Square,
                               accum_out=ss[0:n, jj:jj + 1]).then_inc(s["squared"], 1)
                act.wait_ge(s["squared"], jj + 1)
                if jj == 0 and part == 0:
                    act.wait_ge(cst["eps_set"], 1)
                act.activation(ss[0:n, jj:jj + 1], ss[0:n, jj:jj + 1], ACT.Sqrt, bias=cst["eps"][0:n, :],
                               scale=1.0 / D).then_inc(s["rooted"], 1)
            if part == 0:
                act.wait_ge(s["init"], 1)
            for c in range(QC):
                act.wait_ge(s["proj"], c + 1)
                if c >= 2:
                    act.wait_ge(s["conved"], c - 1)
                act.activation(raw[:, c % 2, 0:CONV - 1], hist[:, c, :], ACT.Copy).then_inc(s["raw_s"], 1)
                act.activation(raw[:, c % 2, CONV - 1:], pp[:, c % 4, 0:TP], ACT.Copy).then_inc(s["raw_s"], 1)
                if c:
                    act.wait_ge(s["conved"], c)
                    act.activation(sT[:, c - 1, 0:TP], sT[:, c - 1, 0:TP], ACT.Silu).then_inc(s["silued"], 1)
                act.wait_ge(s["raw_s"], 2 * c + 2)
                act.activation(hist[:, c, :], raw[:, c % 2, TP:TP + CONV - 1], ACT.Copy).then_inc(s["tail_s"], 1)
                mix.act(act, act_beats.get(c, 0))
            act.wait_ge(s["conved"], QC)
            act.activation(sT[:, QC - 1, 0:TP], sT[:, QC - 1, 0:TP], ACT.Silu).then_inc(s["silued"], 1)
            for m in range(len(jobs)):
                mix.act(act, act_beats.get(QC + m, 0))
            act.wait_ge(s["silued"], QC)
            act.wait_ge(s["tail_s"], QC)

        @block.vector
        def _(dve):
            link = chain(dve, s["dch"])
            if part == 0:
                dve.memset(cst["eps"][:], EPS).then_inc(cst["eps_set"], 1)
                dve.memset(hist[:], 0.0).then_inc(s["init"], 1)
                link(dve.memset(rest[:, 0, :], 0.0))
            dve.wait_ge(s["row_in"], 16)

            def norm(jj):
                n = SIZE[tiles[jj]]
                dve.wait_ge(s["rooted"], jj + 1)
                link(dve.reciprocal(rs[0:n, jj:jj + 1], ss[0:n, jj:jj + 1]))
                dve.scalar_tensor_tensor(out=hs[0:n, jj % 2, :], in0=hx[0:n, jj % 2, :], scalar=rs[0:n, jj:jj + 1],
                                         in1=arow[0:n, :], op0=ALU.mult, op1=ALU.mult).then_inc(s["normed"], 1)

            norm(0)
            for jj, j in enumerate(tiles):
                if jj + 1 < NJ:
                    norm(jj + 1)
                for half in range(2):
                    dve.wait_ge(s["turned"], 2 * jj + half + 1)
                    dve.tensor_copy(hnT[:, 4 * half:4 * half + 4, START[j] - t0:START[j] - t0 + SIZE[j]],
                                    tp[:, half, :].rearrange("p (a b) -> p a b", a=4)[:, :, 0:SIZE[j]]
                                    ).then_inc(s["hnT_s"], 1)
            if part == 0:
                dve.wait_ge(s["cw_mm"], 1)
                dve.tensor_copy(cw[:], tp[:, 0, 0:QC * CONV]).then_inc(s["cw_s"], 1)
                dve.wait_ge(s["cw_s"], 1)
            for c in range(QC):
                dve.wait_ge(s["raw_s"], 2 * c + 2)
                for i in range(CONV):
                    src = raw[:, c % 2, i:i + TP]
                    tap = cw[:, c * CONV + i:c * CONV + i + 1]
                    if i == 0:
                        link(dve.tensor_scalar(sT[:, c, 0:TP], src, tap, None, ALU.mult))
                    else:
                        ins = dve.scalar_tensor_tensor(out=sT[:, c, 0:TP], in0=src, scalar=tap, in1=sT[:, c, 0:TP],
                                                       op0=ALU.mult, op1=ALU.add)
                        if i < CONV - 1:
                            link(ins)
                ins.then_inc(s["conved"], 1)
                mix.dve(dve, beats.get(c, 0))
            for m, (a, jj) in enumerate(jobs):
                dve.wait_ge(s["rest_mm"], m + 1)
                n, width = SIZE[tiles[jj]], min(WCOLS, REST - a * WCOLS)
                dve.tensor_copy(rest[0:n, jj, a * WCOLS:a * WCOLS + width], pp[0:n, m % 4, 0:width]
                                ).then_inc(s["rest_s"], 1)
                mix.dve(dve, beats.get(QC + m, 0))
            dve.wait_ge(s["rest_s"], len(jobs))

        @block.tensor
        def _(pe):
            if part == 0:
                pe.wait_ge(cst["loaded"], 16 * 9)
            for jj, j in enumerate(tiles):
                n = SIZE[j]
                pe.wait_ge(s["normed"], jj + 1)
                for half in range(2):
                    if jj:
                        pe.wait_ge(s["hnT_s"], 2 * jj - 1 + half)
                    for k in range(4):
                        kk = 4 * half + k
                        tr = pe.transpose(tp[:, half, k * P:k * P + n], hs[0:n, jj % 2, kk * P:(kk + 1) * P],
                                          ident[0:n, 0:n])
                    tr.then_inc(s["turned"], 1)
            pe.wait_ge(s["hnT_s"], 2 * NJ)
            if part == 0:
                pe.wait_ge(s["cw_in"], 16)
                for c in range(QC):
                    tr = pe.transpose(tp[:, 0, c * CONV:(c + 1) * CONV], cw4[:, c * P:(c + 1) * P],
                                      ident[0:CONV, 0:CONV])
                tr.then_inc(s["cw_mm"], 1)
            for c in range(QC):
                if c % 2 == 0:
                    w = W.take(pe)
                if c >= 4:
                    pe.wait_ge(s["raw_s"], 2 * (c - 3))
                for k in range(KD):
                    mm = pe.matmul(pp[:, c % 4, 0:TP], w[:, k, (c % 2) * P:(c % 2 + 1) * P], hnT[:, k, :],
                                   start=(k == 0), stop=(k == KD - 1))
                mm.then_inc(s["proj"], 1)
                mix.pe(pe, pe_beats.get(c, 0))
            pe.wait_ge(s["raw_s"], 2 * QC)
            for m, (a, jj) in enumerate(jobs):
                n, width, lo = SIZE[tiles[jj]], min(WCOLS, REST - a * WCOLS), START[tiles[jj]] - t0
                if m == 0 or jobs[m - 1][0] != a:
                    w = W.take(pe)
                if m >= 4:
                    pe.wait_ge(s["rest_s"], m - 3)
                for k in range(KD):
                    mm = pe.matmul(pp[0:n, m % 4, 0:width], hnT[:, k, lo:lo + n], w[:, k, 0:width],
                                   start=(k == 0), stop=(k == KD - 1))
                mm.then_inc(s["rest_mm"], 1)
                mix.pe(pe, pe_beats.get(QC + m, 0))


def delta_rule(nc, dram, cst, keep, mix, part, beats):
    with ExitStack() as ctx:
        t = Tools(nc, ctx)
        act_beats, pe_beats = later(beats, 1), later(beats, 2)
        sT, rest, y = keep["sT"], keep["rest"], keep["y"]
        ident, triu, maskT = cst["ident"], cst["triu"], cst["maskT"]
        levels, pair_ones = cst["levels"], cst["pair_ones"]
        HD = H * DK
        tiles = PARTS[part]
        NJ, t0 = len(tiles), START[tiles[0]]
        TP = sum(SIZE[j] for j in tiles)
        S = keep["S"]
        dtb, alog, grow = t.sb("dtb", [P, H]), t.sb("alog", [P, H]), t.sb("gdn_norm_row", [P, DK])
        xs, ab, e1, u1, l1, g, beta, gc, eg, kds, glE = (t.sb(n, [P, NJ, H]) for n in (
            "xs", "ab", "e1", "u1", "l1", "g", "beta", "gc", "eg", "kds", "glE"))
        glp, bg, orm = t.sb("glp", [P, 4]), t.sb("bg", [P, H]), t.sb("orm", [P, H])
        ones = t.sb("ones", [P, P])
        b1, b2, b3, b4, PT, X, XTr = (t.sb(n, [P, H, P]) for n in ("b1", "b2", "b3", "b4", "PT", "X", "XT"))
        gB, egB, Y = b1, b1, b1
        bB, BT1 = b2, b2
        decT, BT0 = b3, b3
        MT = b4
        sq, inv = (b[:].rearrange("p h i -> p (h i)")[:, 0:2 * TP].rearrange("p (a i) -> p a i", a=2) for b in (b1, b2))
        ktok, vtok = (X[:].rearrange("p h i -> p (h i)")[:, a * HD:(a + 1) * HD] for a in range(2))
        vb, kbg, kd, u, vn = (t.sb(n, [P, HD]) for n in ("vb", "kbg", "kd", "u", "vn"))
        osq, zs = u, vb
        wT, qgT = t.sb("wT", [P, 4, P]), t.sb("qgT", [P, 4, P])
        bank = t.ps("banks", [P, 6, 512])

        def quad(b, n):
            return bank[0:n, b, :].rearrange("p (h i) -> p h i", h=4)

        ORDER = [2 * i + o for o in range(2) for i in range(4)]

        def parity(ap, o):
            return ap.rearrange("p (c o d) -> p o c d", o=2, d=DK)[:, o, :, :]


        names = ("sqd", "normsum", "rooted", "qk_scaled", "turned", "turned_out", "vec_in", "beta_s", "exp_neg",
                 "abs_s", "ln_s", "alog_s", "g_s", "gb_s", "gates_mm", "gc_s", "bcast_mm", "dec_s", "eg_s", "egb_s",
                 "dec_exp", "kk_mm", "mt_s", "qk_mm", "pt_s", "sides_s", "bt_s", "y_mm", "y_out", "xy_mm", "x_s",
                 "uw_mm", "uw_s", "ws_mm", "vn_s", "o_mm", "s_mm", "s_s", "o_out", "osq_s", "osum_s", "oroot",
                 "z_s", "y_s", "ones_s", "dch", "zero_s")
        s = {n: t.sem("b_" + n) for n in names}
        lev = [4 if j == 0 else LEVELS for j in tiles]
        lbase = [2 * sum(lev[:jj]) for jj in range(NJ)]
        ybase = [2 * sum(l - 1 for l in lev[:jj]) for jj in range(NJ)]
        xbase = [sum(4 * (l - 1) + 2 for l in lev[:jj]) for jj in range(NJ)]

        def x_at(jj, l, q):
            return xbase[jj] + 4 * l + ((q + 1) if l == lev[jj] - 1 else 2 * (q + 1))

        live = [jj for jj in range(NJ) if tiles[jj]]
        block = ctx.enter_context(nc.Block())

        @block.sync
        def _(sp):
            sp.dma_start(dtb[:], rows(dram["dt_bias"], P)).then_inc(s["vec_in"], 16)
            sp.dma_start(alog[:], rows(dram["a_log"], P)).then_inc(s["vec_in"], 16)
            sp.dma_start(grow[:], rows(dram["gdn_norm"], P)).then_inc(s["vec_in"], 16)

        @block.gpsimd
        def _(pool):
            mix.pool(pool, sum(beats.values()))

        @block.scalar
        def _(act):
            for c in range(9):
                if c < 8:
                    if c >= 2:
                        act.wait_ge(s["normsum"], c - 1)
                    act.activation(sq[:, c % 2, :], sT[:, c, 0:TP], ACT.Square).then_inc(s["sqd"], 1)
                if c:
                    act.wait_ge(s["normsum"], c)
                    if c >= 3:
                        act.wait_ge(s["qk_scaled"], c - 2)
                    act.activation(inv[:, (c - 1) % 2, :], bank[:, (c - 1) % 4, 0:TP],
                                   ACT.Sqrt, bias=cst["eps"][:]).then_inc(s["rooted"], 1)
                    mix.act(act, act_beats.get(("n", c - 1), 0))
            act.wait_ge(s["vec_in"], 48)
            act.activation(beta[:], rest[:, 0:NJ, B0:B0 + H], ACT.Sigmoid).then_inc(s["beta_s"], 1)
            act.activation(alog[:], alog[:], ACT.Exp).then_inc(s["alog_s"], 1)
            act.wait_ge(s["abs_s"], 1)
            act.activation(e1[:], ab[:], ACT.Exp, scale=-1.0).then_inc(s["exp_neg"], 1)
            act.wait_ge(s["abs_s"], 2)
            act.activation(l1[:], u1[:], ACT.Ln).then_inc(s["ln_s"], 1)
            act.wait_ge(s["alog_s"], 1)
            act.wait_ge(s["gc_s"], 2)
            act.activation(eg[:], gc[:], ACT.Exp).then_inc(s["eg_s"], 1)
            act.activation(kds[:], kds[:], ACT.Exp).then_inc(s["eg_s"], 1)
            act.activation(glE[:], glE[:], ACT.Exp).then_inc(s["eg_s"], 1)
            for jj, j in enumerate(tiles):
                n = SIZE[j]
                if jj:
                    act.wait_ge(s["sides_s"], jj)
                for m in range(2):
                    act.wait_ge(s["turned"], 2 * jj + m + 1)
                    act.activation((ktok if m == 0 else vtok)[0:n, :], bank[0:n, 4 + m, :],
                                   ACT.Copy).then_inc(s["turned_out"], 1)
                act.wait_ge(s["dec_s"], jj + 1)
                act.activation(decT[0:n, :, 0:n], decT[0:n, :, 0:n], ACT.Exp).then_inc(s["dec_exp"], 1)
                for q in range(2):
                    act.activation(egB[:, 4 * q:4 * q + 4, 0:n], quad(q, P)[:, :, 0:n], ACT.Exp).then_inc(s["egb_s"], 1)
                mix.act(act, act_beats.get(("g", jj), 0) + act_beats.get(("a", jj), 0))
                for l in range(1, lev[jj]):
                    for q in range(2):
                        act.wait_ge(s["y_mm"], lbase[jj] + 2 * l + q + 1)
                        act.activation(Y[0:n, 4 * q:4 * q + 4, 0:n], quad(q, n)[:, :, 0:n],
                                       ACT.Copy).then_inc(s["y_out"], 1)
                    mix.act(act, act_beats.get(("l", jj, l), 0))
                act.wait_ge(s["uw_mm"], 2 * jj + 1)
                act.activation(u[0:n, :], bank[0:n, 0, :], ACT.Copy).then_inc(s["uw_s"], 1)
                act.wait_ge(s["uw_mm"], 2 * jj + 2)
                act.activation(wT[:, :, 0:n], quad(1, P)[:, :, 0:n], ACT.Copy).then_inc(s["uw_s"], 1)
                mix.act(act, act_beats.get(("w", jj), 0))
                if j:
                    i = live.index(jj) + 1
                    act.activation(zs[:], rest[:, jj, Z0:Z0 + HD], ACT.Silu).then_inc(s["z_s"], 1)
                    act.wait_ge(s["o_out"], i)
                    act.activation(osq[:], y[:, j - 1, 0:HD], ACT.Square).then_inc(s["osq_s"], 1)
                    act.wait_ge(s["osum_s"], i)
                    act.activation(orm[:], orm[:], ACT.Sqrt, bias=cst["eps"][:],
                                   scale=1.0 / DK).then_inc(s["oroot"], 1)
                    act.wait_ge(s["y_s"], i)
                mix.act(act, act_beats.get(("o", jj), 0))

        @block.vector
        def _(dve):
            link = chain(dve, s["dch"])
            dve.memset(ones[:], 1.0).then_inc(s["ones_s"], 1)
            if part == 0:
                for x in (gc, kds, glE):
                    ins = dve.memset(x[:, 0, :], 0.0)
                link(ins)
            for c in range(8):
                dve.wait_ge(s["rooted"], c + 1)
                link(dve.reciprocal(inv[:, c % 2, :], inv[:, c % 2, :]))
                dve.scalar_tensor_tensor(out=sT[:, c, 0:TP], in0=sT[:, c, 0:TP], scalar=DK ** -0.5 if c < 4 else 1.0,
                                         in1=inv[:, c % 2, :], op0=ALU.mult, op1=ALU.mult).then_inc(s["qk_scaled"], 1)
                mix.dve(dve, beats.get(("n", c), 0))
            dve.wait_ge(s["vec_in"], 48)
            link(dve.tensor_tensor(xs[:], rest[:, 0:NJ, A0:A0 + H], dtb[:].unsqueeze(1).to_broadcast([P, NJ, H]),
                                   ALU.add))
            dve.scalar_tensor_tensor(out=ab[:], in0=xs[:], scalar=-1.0, in1=xs[:], op0=ALU.mult,
                                     op1=ALU.max).then_inc(s["abs_s"], 1)
            dve.wait_ge(s["exp_neg"], 1)
            dve.tensor_scalar(u1[:], e1[:], 1.0, None, ALU.add).then_inc(s["abs_s"], 1)
            dve.wait_ge(s["abs_s"], 2)
            link(dve.scalar_tensor_tensor(out=e1[:], in0=u1[:], scalar=-1.0, in1=e1[:], op0=ALU.add, op1=ALU.subtract))
            dve.wait_ge(s["ln_s"], 1)
            link(dve.reciprocal(u1[:], u1[:]))
            link(dve.tensor_tensor(e1[:], e1[:], u1[:], ALU.mult))
            link(dve.tensor_tensor(l1[:], l1[:], e1[:], ALU.subtract))
            link(dve.scalar_tensor_tensor(out=l1[:], in0=xs[:], scalar=0.0, in1=l1[:], op0=ALU.max, op1=ALU.add))
            dve.wait_ge(s["alog_s"], 1)
            dve.scalar_tensor_tensor(out=g[:], in0=l1[:], scalar=-1.0,
                                     in1=alog[:].unsqueeze(1).to_broadcast([P, NJ, H]),
                                     op0=ALU.mult, op1=ALU.mult).then_inc(s["g_s"], 1)
            dve.wait_ge(s["g_s"], 1)
            dve.wait_ge(s["beta_s"], 1)
            dve.wait_ge(s["gates_mm"], 1)
            for jj, j in enumerate(tiles):
                n = SIZE[j]
                ins = dve.tensor_copy(gc[0:n, jj, :], bank[0:n, 4, 32 * jj:32 * jj + H])
                ins = dve.tensor_copy(glE[:, jj, :], bank[:, 4, 32 * jj + 16:32 * jj + 16 + H])
            ins.then_inc(s["gc_s"], 1)
            dve.wait_ge(s["gc_s"], 1)
            for jj, j in enumerate(tiles):
                n = SIZE[j]
                ins = dve.tensor_tensor(kds[0:n, jj, :], glE[0:n, jj, :], gc[0:n, jj, :], ALU.subtract)
            ins.then_inc(s["gc_s"], 1)
            dve.wait_ge(s["eg_s"], 3)
            for jj, j in enumerate(tiles):
                n = SIZE[j]
                if jj:
                    dve.wait_ge(s["y_out"], ybase[jj])
                else:
                    dve.wait_ge(s["qk_scaled"], 8)
                for o in range(2):
                    hs = slice(4 * o, 4 * o + 4)
                    dve.tensor_copy(gB[0:n, hs, :], g[0:n, jj, o::2].unsqueeze(2).to_broadcast([n, 4, P])
                                    ).then_inc(s["gb_s"], 1)
                    dve.tensor_copy(bB[0:n, hs, :], beta[0:n, jj, o::2].unsqueeze(2).to_broadcast([n, 4, P])
                                    ).then_inc(s["gb_s"], 1)
                dve.wait_ge(s["bcast_mm"], jj + 1)
                for m, h in enumerate(ORDER):
                    ins = dve.scalar_tensor_tensor(out=decT[0:n, m, 0:n], in0=quad(m // 4, n)[:, m % 4, 0:n],
                                                   scalar=gc[0:n, jj, h:h + 1], in1=maskT[0:n, 0:n],
                                                   op0=ALU.subtract, op1=ALU.add)
                ins.then_inc(s["dec_s"], 1)
                link(dve.tensor_tensor(bg[0:n, :], beta[0:n, jj, :], eg[0:n, jj, :], ALU.mult))
                dve.wait_ge(s["turned_out"], 2 * jj + 2)

                def by_head(out, src, col):
                    return dve.tensor_tensor(out[0:n, :].rearrange("p (h d) -> p h d", h=H),
                                             src[0:n, :].rearrange("p (h d) -> p h d", h=H),
                                             col.unsqueeze(2).to_broadcast([n, H, DK]), ALU.mult)
                by_head(vb, vtok, beta[0:n, jj, :])
                by_head(kbg, ktok, bg[0:n, :])
                link(by_head(kd, ktok, kds[0:n, jj, :]))
                mix.dve(dve, beats.get(("g", jj), 0))
                dve.wait_ge(s["dec_exp"], jj + 1)
                dve.wait_ge(s["kk_mm"], 2 * jj + 2)
                for q in range(2):
                    hs = slice(4 * q, 4 * q + 4)
                    ins = dve.tensor_tensor(MT[0:n, hs, 0:n], quad(4 + q, n)[:, :, 0:n], decT[0:n, hs, 0:n], ALU.mult)
                link(ins)
                for q in range(2):
                    hs = slice(4 * q, 4 * q + 4)
                    dve.tensor_tensor(MT[0:n, hs, 0:n], MT[0:n, hs, 0:n], quad(2 + q, n)[:, :, 0:n],
                                      ALU.mult).then_inc(s["mt_s"], 1)
                dve.wait_ge(s["egb_s"], 2 * jj + 2)
                for o in (0, 1):
                    r = slice(64 * o, 64 * o + 64)
                    dve.tensor_copy(glp[r, :], glE[r, jj, o::2])
                    ins = dve.tensor_tensor(qgT[r, :, 0:n], sT[r, 0:4, START[j] - t0:START[j] - t0 + n],
                                            egB[r, 4 * o:4 * o + 4, 0:n], ALU.mult)
                ins.then_inc(s["sides_s"], 1)
                dve.wait_ge(s["sides_s"], jj + 1)
                for q in range(2):
                    hs = slice(4 * q, 4 * q + 4)
                    dve.wait_ge(s["qk_mm"], 2 * jj + q + 1)
                    dve.tensor_tensor(PT[0:n, hs, 0:n], quad(q, n)[:, :, 0:n], decT[0:n, hs, 0:n],
                                      ALU.mult).then_inc(s["pt_s"], 1)
                dve.wait_ge(s["mt_s"], 2 * jj + 2)
                dve.wait_ge(s["pt_s"], 2 * jj + 2)
                mix.dve(dve, beats.get(("a", jj), 0))

                def blocks(l):
                    for q in range(2):
                        hs = slice(4 * q, 4 * q + 4)
                        dve.tensor_tensor((BT0, BT1)[l % 2][0:n, hs, 0:n], MT[0:n, hs, 0:n],
                                          levels[0:n, l, 0:n].unsqueeze(1).to_broadcast([n, 4, n]),
                                          ALU.mult).then_inc(s["bt_s"], 1)

                blocks(0)
                for l in range(lev[jj]):
                    if l + 1 < lev[jj]:
                        blocks(l + 1)
                    for q in range(2):
                        hs = slice(4 * q, 4 * q + 4)
                        if l == 0:
                            idb = ident[0:n, 0:n].unsqueeze(1).to_broadcast([n, 4, n])
                            dve.wait_ge(s["bt_s"], lbase[jj] + 2)
                            dve.tensor_tensor(XTr[0:n, hs, 0:n], idb, BT0[0:n, hs, 0:n], ALU.subtract
                                              ).then_inc(s["x_s"], 1)
                            dve.wait_ge(s["y_mm"], lbase[jj] + q + 1)
                            dve.tensor_tensor(X[0:n, hs, 0:n], idb, quad(q, n)[:, :, 0:n], ALU.subtract
                                              ).then_inc(s["x_s"], 1)
                            continue
                        dve.wait_ge(s["xy_mm"], ybase[jj] + 2 * (l - 1) + q + 1)
                        if l < lev[jj] - 1:
                            dve.tensor_tensor(X[0:n, hs, 0:n], X[0:n, hs, 0:n], quad(2 + q, n)[:, :, 0:n],
                                              ALU.subtract).then_inc(s["x_s"], 1)
                        dve.tensor_tensor(XTr[0:n, hs, 0:n], XTr[0:n, hs, 0:n], quad(4 + q, n)[:, :, 0:n],
                                          ALU.subtract).then_inc(s["x_s"], 1)
                    dve.wait_ge(s["x_s"], x_at(jj, l, 1))
                    if l:
                        mix.dve(dve, beats.get(("l", jj, l), 0))
                dve.wait_ge(s["uw_s"], 2 * jj + 2)
                if j == 0:
                    dve.tensor_copy(vn[0:n, :], u[0:n, :]).then_inc(s["vn_s"], 1)
                else:
                    i = live.index(jj) + 1
                    dve.wait_ge(s["ws_mm"], i)
                    for o, b in ((0, 2), (1, 3)):
                        ins = dve.tensor_tensor(parity(vn[0:n, :], o), parity(u[0:n, :], o),
                                                bank[0:n, b, 0:256].rearrange("p (c d) -> p c d", c=4), ALU.subtract)
                    ins.then_inc(s["vn_s"], 1)
                mix.dve(dve, beats.get(("w", jj), 0))
                dve.wait_ge(s["s_mm"], jj + 1)
                upd = bank[:, 4, 0:4 * DK].rearrange("p (c e) -> p c e", c=4)
                if j == 0:
                    dve.tensor_copy(S[:], upd).then_inc(s["s_s"], 1)
                else:
                    link(dve.tensor_tensor(S[:], S[:], glp[:].unsqueeze(2).to_broadcast([P, 4, DK]), ALU.mult))
                    dve.tensor_tensor(S[:], S[:], upd, ALU.add).then_inc(s["s_s"], 1)
                    yo = y[:, j - 1, 0:HD]
                    yh = yo.rearrange("p (h d) -> p h d", h=H)
                    for o, b in ((0, 2), (1, 5)):
                        ins = dve.tensor_copy(parity(yo, o), bank[:, b, 0:256].rearrange("p (c d) -> p c d", c=4))
                    ins.then_inc(s["o_out"], 1)
                    dve.wait_ge(s["osq_s"], i)
                    dve.tensor_reduce(orm[:], osq[:].rearrange("p (h d) -> p h d", h=H), AX,
                                      ALU.add).then_inc(s["osum_s"], 1)
                    dve.wait_ge(s["oroot"], i)
                    link(dve.reciprocal(orm[:], orm[:]))
                    link(dve.tensor_tensor(yh, yh, orm[:].unsqueeze(2).to_broadcast([P, H, DK]), ALU.mult))
                    link(dve.tensor_tensor(yh, yh, grow[:].unsqueeze(1).to_broadcast([P, H, DK]), ALU.mult))
                    dve.tensor_tensor(yo, yo, zs[:], ALU.mult).then_inc(s["y_s"], 1)
                    dve.wait_ge(s["y_s"], i)
                dve.wait_ge(s["s_s"], jj + 1)
                mix.dve(dve, beats.get(("o", jj), 0))

        @block.tensor
        def _(pe):
            pe.wait_ge(s["ones_s"], 1)
            for c in range(8):
                pe.wait_ge(s["sqd"], c + 1)
                if c >= 4:
                    pe.wait_ge(s["rooted"], c - 3)
                pe.matmul(bank[:, c % 4, 0:TP], pair_ones[:], sq[:, c % 2, :], start=True, stop=True
                          ).then_inc(s["normsum"], 1)
                if c:
                    mix.pe(pe, pe_beats.get(("n", c - 1), 0))
            mix.pe(pe, pe_beats.get(("n", 7), 0))
            pe.wait_ge(s["qk_scaled"], 8)
            pe.wait_ge(s["g_s"], 1)
            pe.wait_ge(s["rooted"], 8)
            for jj, j in enumerate(tiles):
                n = SIZE[j]
                pe.matmul(bank[0:n, 4, 32 * jj:32 * jj + H], triu[0:n, 0:n], g[0:n, jj, :], start=True, stop=True)
                mm = pe.matmul(bank[:, 4, 32 * jj + 16:32 * jj + 16 + H], ones[0:n, :], g[0:n, jj, :],
                               start=True, stop=True)
            mm.then_inc(s["gates_mm"], 1)
            pe.wait_ge(s["gc_s"], 1)
            for jj, j in enumerate(tiles):
                n, cols = SIZE[j], slice(START[j] - t0, START[j] - t0 + SIZE[j])
                if jj:
                    pe.wait_ge(s["s_s"], jj)
                    if tiles[jj - 1]:
                        pe.wait_ge(s["o_out"], live.index(jj - 1) + 1)
                for m in range(2):
                    for c in range(4):
                        tr = pe.transpose(bank[0:n, 4 + m, c * P:(c + 1) * P], sT[:, 4 + 4 * m + c, cols], ident[:])
                    tr.then_inc(s["turned"], 1)
                pe.wait_ge(s["gb_s"], 4 * jj + 4)
                for h in range(H):
                    pe.matmul(quad(h // 4, P)[:, h % 4, 0:n], gB[0:n, h, :], triu[0:n, 0:n], start=True, stop=True)
                for h in range(H):
                    mm = pe.matmul(quad(2 + h // 4, P)[:, h % 4, 0:n], bB[0:n, h, :], ident[0:n, 0:n],
                                   start=True, stop=True)
                mm.then_inc(s["bcast_mm"], 1)
                pe.wait_ge(s["turned_out"], 2 * jj + 2)
                for m, h in enumerate(ORDER):
                    r = slice(64 * (h % 2), 64 * (h % 2) + 64)
                    mm = pe.matmul(quad(4 + m // 4, n)[:, m % 4, 0:n], sT[r, 4 + h // 2, cols], sT[r, 4 + h // 2, cols],
                                   start=True, stop=True)
                    if m % 4 == 3:
                        mm.then_inc(s["kk_mm"], 1)
                mix.pe(pe, pe_beats.get(("g", jj), 0))
                pe.wait_ge(s["egb_s"], 2 * jj + 2)
                pe.wait_ge(s["dec_s"], jj + 1)
                for m, h in enumerate(ORDER):
                    r = slice(64 * (h % 2), 64 * (h % 2) + 64)
                    mm = pe.matmul(quad(m // 4, n)[:, m % 4, 0:n], sT[r, 4 + h // 2, cols], sT[r, h // 2, cols],
                                   start=True, stop=True)
                    if m % 4 == 3:
                        mm.then_inc(s["qk_mm"], 1)
                pe.wait_ge(s["mt_s"], 2 * jj + 2)
                pe.wait_ge(s["pt_s"], 2 * jj + 2)
                mix.pe(pe, pe_beats.get(("a", jj), 0))
                for l in range(lev[jj]):
                    BT = (BT0, BT1)[l % 2]
                    for q in range(2):
                        pe.wait_ge(s["bt_s"], lbase[jj] + 2 * l + q + 1)
                        if l:
                            pe.wait_ge(s["x_s"], x_at(jj, l - 1, q))
                        for h in range(4 * q, 4 * q + 4):
                            mm = pe.matmul(quad(q, n)[:, h % 4, 0:n], BT[0:n, h, 0:n],
                                           X[0:n, h, 0:n] if l else ident[0:n, 0:n], start=True, stop=True)
                        mm.then_inc(s["y_mm"], 1)
                    if l == 0:
                        continue
                    for q in range(2):
                        pe.wait_ge(s["y_out"], ybase[jj] + 2 * (l - 1) + q + 1)
                        if l < lev[jj] - 1:
                            for h in range(4 * q, 4 * q + 4):
                                pe.matmul(quad(2 + q, n)[:, h % 4, 0:n], XTr[0:n, h, 0:n], Y[0:n, h, 0:n],
                                          start=True, stop=True)
                        for h in range(4 * q, 4 * q + 4):
                            mm = pe.matmul(quad(4 + q, n)[:, h % 4, 0:n], Y[0:n, h, 0:n], XTr[0:n, h, 0:n],
                                           start=True, stop=True)
                        mm.then_inc(s["xy_mm"], 1)
                    mix.pe(pe, pe_beats.get(("l", jj, l), 0))
                pe.wait_ge(s["x_s"], x_at(jj, lev[jj] - 1, 1))
                pe.wait_ge(s["sides_s"], jj + 1)
                for m, h in enumerate(ORDER):
                    mm = pe.matmul(bank[0:n, 0, h * DK:(h + 1) * DK], XTr[0:n, m, 0:n], vb[0:n, h * DK:(h + 1) * DK],
                                   start=True, stop=True)
                mm.then_inc(s["uw_mm"], 1)
                for m, h in enumerate(ORDER):
                    r = slice(64 * (h % 2), 64 * (h % 2) + 64)
                    mm = pe.matmul(quad(1, P)[r, h // 2, 0:n], kbg[0:n, h * DK:(h + 1) * DK], XTr[0:n, m, 0:n],
                                   start=True, stop=True)
                mm.then_inc(s["uw_mm"], 1)
                if j:
                    pe.wait_ge(s["uw_s"], 2 * jj + 2)
                    for h in range(H):
                        r = slice(64 * (h % 2), 64 * (h % 2) + 64)
                        mm = pe.matmul(bank[0:n, (2, 3)[h % 2], (h // 2) * DK:(h // 2 + 1) * DK], wT[r, h // 2, 0:n],
                                       S[r, h // 2, :], start=True, stop=True)
                    mm.then_inc(s["ws_mm"], 1)
                mix.pe(pe, pe_beats.get(("w", jj), 0))
                pe.wait_ge(s["vn_s"], jj + 1)
                if j:
                    for m, h in enumerate(ORDER):
                        r = slice(64 * (h % 2), 64 * (h % 2) + 64)
                        o = bank[0:n, (2, 5)[h % 2], (h // 2) * DK:(h // 2 + 1) * DK]
                        pe.matmul(o, qgT[r, h // 2, 0:n], S[r, h // 2, :], start=True, stop=False)
                        mm = pe.matmul(o, PT[0:n, m, 0:n], vn[0:n, h * DK:(h + 1) * DK], start=False, stop=True)
                    mm.then_inc(s["o_mm"], 1)
                for h in range(H):
                    r = slice(64 * (h % 2), 64 * (h % 2) + 64)
                    mm = pe.matmul(bank[r, 4, (h // 2) * DK:(h // 2) * DK + DK], kd[0:n, h * DK:(h + 1) * DK],
                                   vn[0:n, h * DK:(h + 1) * DK], start=True, stop=True)
                mm.then_inc(s["s_mm"], 1)
                mix.pe(pe, pe_beats.get(("o", jj), 0))


def latent_attention(nc, dram, cst, keep, mix, part, beats):
    with ExitStack() as ctx:
        t = Tools(nc, ctx)
        act_beats, pe_beats = later(beats, 1), later(beats, 2)
        rest, y, ident, mask = keep["rest"], keep["y"], cst["ident"], cst["mask"]
        LAT, VD = QL + KL, 64
        tiles = PARTS[part]
        NJ = len(tiles)
        kT, V = keep["kT"], keep["V"]
        wuq, wukv = t.sb("w_uq_s", [P, 2, H * QKD]), t.sb("w_ukv_s", [P, H * P])
        lrow, nrow = t.sb("latent_rows", [P, LAT]), t.sb("head_rows", [P, 2, QKD])
        ls, junk = t.sb("ls", [P, 2 * NJ]), t.sb("lat_junk", [P, LAT])
        cn = t.sb("cn", [P, LAT])
        cT = t.sb("cT", [P, 3, P])
        QKs, QKsq = t.sb("QK", [P, 2, 2, H, QKD]), t.sb("QKsq", [P, 2, H, QKD])
        qks = t.sb("qks", [P, 2, H])
        ra, rb = t.sb("ra", [P, 2, H, 16]), t.sb("rb", [P, 2, H, 16])
        rc, rd = t.sb("rc", [P, 2, H, 16]), t.sb("rd", [P, 2, H, 16])
        qT = t.sb("qT", [QKD, H, 2 * P])
        nm, mx, rsum = t.sb("nm", [P, 2]), t.sb("mx", [P, 2]), t.sb("rsum", [P, 2, H])
        rinv = t.sb("rinv", [P, H])
        pm, pT = t.sb("probs", [P, 2, T]), t.sb("probsT", [P, 2, NT, P])
        bank = t.ps("mla_banks", [P, 6, 512])
        names = ("w_in", "lsq", "lroot", "cn_s", "ct_mm", "ct_s", "qkv_mm", "qk_s", "v_s", "qk_sq", "qk_sum",
                 "qk_root", "qk_norm", "rope_s", "tr_mm", "tr_s", "s_mm", "max_s", "exp_s", "pt_mm", "pt_s",
                 "o_mm", "o_s", "dch", "prep")
        s = {n: t.sem("c_" + n) for n in names}
        units = [(j, h) for j in tiles if j for h in range(H)]
        xt = [j for j in tiles if j]
        KCOL = lambda j: SEQ if j == 0 else (j - 1) * P
        turns = [(jj, side, q) for jj, j in enumerate(tiles) for side in ((1,) if j == 0 else (0, 1)) for q in range(2)]
        upto = [sum(1 for x in turns if x[0] <= jj) for jj in range(NJ)]
        ropes = [sum(1 if j == 0 else 2 for j in tiles[:jj + 1]) for jj in range(NJ)]
        block = ctx.enter_context(nc.Block())

        @block.sync
        def _(sp):
            sp.dma_start(wuq[:], dram["w_uq"].rearrange("(k p) n -> p k n", p=P)).then_inc(s["w_in"], 16)
            sp.dma_start(wukv[:], dram["w_ukv"]).then_inc(s["w_in"], 16)
            sp.dma_start(lrow[:, 0:QL], rows(dram["q_a_norm"], P)).then_inc(s["w_in"], 16)
            sp.dma_start(lrow[:, QL:LAT], rows(dram["kv_a_norm"], P)).then_inc(s["w_in"], 16)
            sp.dma_start(nrow[:, 0, :], rows(dram["q_norm"], P)).then_inc(s["w_in"], 16)
            sp.dma_start(nrow[:, 1, :], rows(dram["k_norm"], P)).then_inc(s["w_in"], 16)

        @block.gpsimd
        def _(pool):
            mix.pool(pool, sum(beats.values()))

        @block.scalar
        def _(act):
            link = chain(act, s["lsq"])
            for jj, j in enumerate(tiles):
                n = SIZE[j]
                link(act.activation(junk[0:n, 0:QL], rest[0:n, jj, CQ0:CQ0 + QL], ACT.Square,
                                    accum_out=ls[0:n, 2 * jj:2 * jj + 1]))
                link(act.activation(junk[0:n, QL:LAT], rest[0:n, jj, CKV0:CKV0 + KL], ACT.Square,
                                    accum_out=ls[0:n, 2 * jj + 1:2 * jj + 2]))
                act.activation(ls[0:n, 2 * jj:2 * jj + 1], ls[0:n, 2 * jj:2 * jj + 1], ACT.Sqrt, bias=cst["eps"][0:n, :],
                               scale=1.0 / QL).then_inc(s["lroot"], 1)
                act.activation(ls[0:n, 2 * jj + 1:2 * jj + 2], ls[0:n, 2 * jj + 1:2 * jj + 2], ACT.Sqrt,
                               bias=cst["eps"][0:n, :], scale=1.0 / KL).then_inc(s["lroot"], 1)
            for jj, j in enumerate(tiles):
                n, lo, QK = SIZE[j], (1 if j == 0 else 0), QKs[:, jj % 2, :, :, :]
                act.wait_ge(s["qkv_mm"], jj + 1)
                if jj >= 2:
                    act.wait_ge(s["tr_mm"], upto[jj - 2])
                if j:
                    link(act.activation(QK[0:n, 0, :, :].rearrange("p h d -> p (h d)").rearrange("p (a c) -> p a c", a=2),
                                        bank[0:n, 0:2, 0:384], ACT.Copy))
                kv = bank[0:n, 2:4, :].rearrange("p a (h d) -> p (a h) d", d=P)
                link(act.activation(QK[0:n, 1, :, 0:NOPE], kv[:, :, 0:NOPE], ACT.Copy))
                act.activation(V[0:n, j, :, :], kv[:, :, NOPE:P], ACT.Copy).then_inc(s["v_s"], 1)
                link(act.activation(QK[0:n, 1, :, NOPE:QKD],
                                    rest[0:n, jj, KPE0:KPE0 + ROPE].unsqueeze(1).to_broadcast([n, H, ROPE]), ACT.Copy))
                act.activation(QKsq[0:n, lo:, :, :], QK[0:n, lo:, :, :], ACT.Square).then_inc(s["qk_sq"], 1)
                act.wait_ge(s["qk_sum"], jj + 1)
                act.activation(qks[0:n, lo:, :], qks[0:n, lo:, :], ACT.Sqrt, bias=cst["eps"][0:n, :],
                               scale=1.0 / QKD).then_inc(s["qk_root"], 1)
                mix.act(act, act_beats.get(("t", jj), 0))
            for i in range(len(units) + 1):
                if i:
                    tt, h = units[i - 1]
                    act.wait_ge(s["pt_mm"], i)
                    if i >= 3:
                        act.wait_ge(s["o_mm"], i - 2)
                    act.activation(pT[:, (i - 1) % 2, 0:tt, :], bank[:, 4, 0:P * tt].rearrange("p (a b) -> p a b", b=P),
                                   ACT.Copy).then_inc(s["pt_s"], 1)
                    act.activation(pT[0:META, (i - 1) % 2, NT - 1, :], bank[0:META, 2 * ((i - 1) % 2) + 1, 256:256 + P],
                                   ACT.Copy).then_inc(s["pt_s"], 1)
                if i < len(units):
                    tt, h = units[i]
                    act.wait_ge(s["max_s"], i + 1)
                    if i >= 2:
                        act.wait_ge(s["pt_mm"], i - 1)
                    act.activation(pm[:, i % 2, 0:P * tt + META], bank[:, 2 * (i % 2):2 * (i % 2) + 2, :].rearrange(
                        "p a b -> p (a b)")[:, 0:P * tt + META], ACT.Exp, bias=nm[:, i % 2:i % 2 + 1], scale=SCALE,
                        accum_out=rsum[:, tt % 2, h:h + 1]).then_inc(s["exp_s"], 1)
                if i:
                    mix.act(act, act_beats.get(("u", i - 1), 0))

        @block.vector
        def _(dve):
            link = chain(dve, s["dch"])
            dve.wait_ge(s["w_in"], 96)

            def latent(jj):
                n = SIZE[tiles[jj]]
                dve.wait_ge(s["lroot"], 2 * jj + 2)
                link(dve.reciprocal(ls[0:n, 2 * jj:2 * jj + 2], ls[0:n, 2 * jj:2 * jj + 2]))
                if jj:
                    dve.wait_ge(s["ct_mm"], jj)
                dve.scalar_tensor_tensor(out=cn[0:n, 0:QL], in0=rest[0:n, jj, CQ0:CQ0 + QL],
                                         scalar=ls[0:n, 2 * jj:2 * jj + 1], in1=lrow[0:n, 0:QL],
                                         op0=ALU.mult, op1=ALU.mult).then_inc(s["cn_s"], 1)
                dve.scalar_tensor_tensor(out=cn[0:n, QL:LAT], in0=rest[0:n, jj, CKV0:CKV0 + KL],
                                         scalar=ls[0:n, 2 * jj + 1:2 * jj + 2], in1=lrow[0:n, QL:LAT],
                                         op0=ALU.mult, op1=ALU.mult).then_inc(s["cn_s"], 1)

            def latent_out(jj):
                n = SIZE[tiles[jj]]
                dve.wait_ge(s["ct_mm"], jj + 1)
                if jj:
                    dve.wait_ge(s["qkv_mm"], jj)
                dve.tensor_copy(cT[:, :, 0:n], bank[:, 4, 0:3 * P].rearrange("p (a b) -> p a b", a=3)[:, :, 0:n]
                                ).then_inc(s["ct_s"], 1)

            latent(0)
            latent_out(0)
            done = 0
            for jj, j in enumerate(tiles):
                n, lo, QK = SIZE[j], (1 if j == 0 else 0), QKs[:, jj % 2, :, :, :]
                if jj + 1 < NJ:
                    latent(jj + 1)
                    latent_out(jj + 1)
                hs = slice(lo, 2)
                dve.wait_ge(s["qk_sq"], jj + 1)
                dve.tensor_reduce(qks[0:n, hs, :], QKsq[0:n, hs, :, :], AX, ALU.add).then_inc(s["qk_sum"], 1)
                dve.wait_ge(s["qk_root"], jj + 1)
                link(dve.reciprocal(qks[0:n, hs, :], qks[0:n, hs, :]))
                for side in range(lo, 2):
                    link(dve.tensor_tensor(QK[0:n, side, :, :], QK[0:n, side, :, :],
                                           qks[0:n, side, :].unsqueeze(2).to_broadcast([n, H, QKD]), ALU.mult))
                    link(dve.tensor_tensor(QK[0:n, side, :, :], QK[0:n, side, :, :],
                                           nrow[0:n, side, :].unsqueeze(1).to_broadcast([n, H, QKD]), ALU.mult))
                    cos = cst["cos"][0:n, j, :].unsqueeze(1).to_broadcast([n, H, 16])
                    sin = cst["sin"][0:n, j, :].unsqueeze(1).to_broadcast([n, H, 16])
                    x1, x2 = QK[0:n, side, :, NOPE:NOPE + 16], QK[0:n, side, :, NOPE + 16:QKD]
                    dve.tensor_tensor(ra[0:n, side, :, :], x1, cos, ALU.mult)
                    dve.tensor_tensor(rb[0:n, side, :, :], x2, sin, ALU.mult)
                    dve.tensor_tensor(rc[0:n, side, :, :], x2, cos, ALU.mult)
                    link(dve.tensor_tensor(rd[0:n, side, :, :], x1, sin, ALU.mult))
                    dve.tensor_tensor(x1, ra[0:n, side, :, :], rb[0:n, side, :, :], ALU.subtract)
                    dve.tensor_tensor(x2, rc[0:n, side, :, :], rd[0:n, side, :, :], ALU.add).then_inc(s["rope_s"], 1)
                for side in range(lo, 2):
                    for q in range(2):
                        dve.wait_ge(s["tr_mm"], done + 1)
                        dst = (kT if side else qT)[:, 4 * q:4 * q + 4, :]
                        c0 = KCOL(j) if side else P * (jj - NJ + 2)
                        dve.tensor_copy(dst[:, :, c0:c0 + n],
                                        bank[0:QKD, 4 + done % 2, :].rearrange("p (a b) -> p a b", a=4)[:, :, 0:n]
                                        ).then_inc(s["tr_s"], 1)
                        done += 1
                mix.dve(dve, beats.get(("t", jj), 0))
            for i, (tt, h) in enumerate(units):
                sc = bank[:, 2 * (i % 2):2 * (i % 2) + 2, :].rearrange("p a b -> p (a b)")
                dve.wait_ge(s["s_mm"], i + 1)
                if i >= 2:
                    dve.wait_ge(s["exp_s"], i - 1)
                diag = sc[:, P * (tt - 1):P * tt]
                link(dve.tensor_tensor(diag, diag, mask[:], ALU.add))
                link(dve.tensor_reduce(mx[:, i % 2:i % 2 + 1], sc[:, 0:P * tt + META], AX, ALU.max))
                dve.tensor_scalar(nm[:, i % 2:i % 2 + 1], mx[:, i % 2:i % 2 + 1], -SCALE, None,
                                  ALU.mult).then_inc(s["max_s"], 1)
                if i:
                    mix.dve(dve, beats.get(("u", i - 1), 0))
                if (h == 0 and i) or i == len(units) - 1:
                    td = units[i - 1][0] if h == 0 else tt
                    done_units = H * (xt.index(td) + 1)
                    dve.wait_ge(s["o_mm"], done_units)
                    dve.wait_ge(s["exp_s"], done_units)
                    link(dve.reciprocal(rinv[:], rsum[:, td % 2, :]))
                    dve.tensor_tensor(y[:, td - 1, 512:D].rearrange("p (h d) -> p h d", h=H),
                                      bank[:, 5, :].rearrange("p (h d) -> p h d", h=H),
                                      rinv[:].unsqueeze(2).to_broadcast([P, H, VD]), ALU.mult).then_inc(s["o_s"], 1)
                    dve.wait_ge(s["o_s"], xt.index(td) + 1)
            mix.dve(dve, beats.get(("u", len(units) - 1), 0))

        @block.tensor
        def _(pe):
            pe.wait_ge(s["w_in"], 96)
            done = 0

            def expand(jj):
                n, j = SIZE[tiles[jj]], tiles[jj]
                pe.wait_ge(s["cn_s"], 2 * jj + 2)
                if jj >= 2:
                    pe.wait_ge(s["tr_s"], upto[jj - 2])
                for c in range(3):
                    tr = pe.transpose(bank[:, 4, c * P:c * P + n], cn[0:n, c * P:(c + 1) * P], ident[0:n, 0:n])
                tr.then_inc(s["ct_mm"], 1)
                pe.wait_ge(s["ct_s"], jj + 1)
                if jj:
                    pe.wait_ge(s["qk_sq"], jj)
                    pe.wait_ge(s["v_s"], jj)
                if j:
                    for a in range(2):
                        for c in range(2):
                            pe.matmul(bank[0:n, a, 0:384], cT[:, c, 0:n], wuq[:, c, 384 * a:384 * a + 384],
                                      start=(c == 0), stop=(c == 1))
                for a in range(2):
                    mm = pe.matmul(bank[0:n, 2 + a, :], cT[:, 2, 0:n], wukv[:, 512 * a:512 * a + 512],
                                   start=True, stop=True)
                mm.then_inc(s["qkv_mm"], 1)

            expand(0)
            for jj, j in enumerate(tiles):
                if jj + 1 < NJ:
                    expand(jj + 1)
                n, QK = SIZE[j], QKs[:, jj % 2, :, :, :]
                lo = 1 if j == 0 else 0
                pe.wait_ge(s["rope_s"], ropes[jj])
                for side in range(lo, 2):
                    for q in range(2):
                        if done >= 2:
                            pe.wait_ge(s["tr_s"], done - 1)
                        for h in range(4):
                            tr = pe.transpose(bank[0:QKD, 4 + done % 2, h * P:h * P + n], QK[0:n, side, 4 * q + h, :],
                                              ident[0:n, 0:n])
                        tr.then_inc(s["tr_mm"], 1)
                        done += 1
                mix.pe(pe, pe_beats.get(("t", jj), 0))
            pe.wait_ge(s["tr_s"], len(turns))
            pe.wait_ge(s["v_s"], NJ)

            def score(i):
                tt, h = units[i]
                if i >= 2:
                    pe.wait_ge(s["exp_s"], i - 1)
                q = qT[:, h, P * xt.index(tt):P * (xt.index(tt) + 1)]
                b0, off = (2 * (i % 2), P * tt) if tt < XT else (2 * (i % 2) + 1, 0)
                pe.matmul(bank[:, 2 * (i % 2), 0:P * tt], q, kT[:, h, 0:P * tt], start=True, stop=True)
                pe.matmul(bank[:, b0, off:off + META], q, kT[:, h, SEQ:T], start=True, stop=True).then_inc(s["s_mm"], 1)

            score(0)
            for i, (tt, h) in enumerate(units):
                if i + 1 < len(units):
                    score(i + 1)
                pe.wait_ge(s["exp_s"], i + 1)
                if i:
                    pe.wait_ge(s["pt_s"], 2 * i)
                for c in range(tt):
                    pe.transpose(bank[:, 4, c * P:(c + 1) * P], pm[:, i % 2, c * P:(c + 1) * P], ident[:])
                pe.transpose(bank[0:META, 2 * (i % 2) + 1, 256:256 + P], pm[:, i % 2, P * tt:P * tt + META], ident[:]).then_inc(s["pt_mm"], 1)
                n = pe_beats.get(("u", i), 0)
                mix.pe(pe, n // 2)
                pe.wait_ge(s["pt_s"], 2 * i + 2)
                if h == 0 and i:
                    pe.wait_ge(s["o_s"], xt.index(tt))
                o = bank[:, 5, h * VD:(h + 1) * VD]
                for c in range(tt):
                    pe.matmul(o, pT[:, i % 2, c, :], V[:, c + 1, h, :], start=(c == 0), stop=False)
                pe.matmul(o, pT[0:META, i % 2, NT - 1, :], V[0:META, 0, h, :], start=False, stop=True
                          ).then_inc(s["o_mm"], 1)
                mix.pe(pe, n - n // 2)


def out_project(nc, dram, cst, y, h1, W, mix, part, beats):
    with ExitStack() as ctx:
        t = Tools(nc, ctx)
        act_beats, pe_beats = later(beats, 1), later(beats, 2)
        ident = cst["ident"]
        xt = [j - 1 for j in PARTS[part] if j]
        N, NB = len(xt), D // WCOLS
        yT, frow, fs = t.sb("yT", [P, N, KD, P]), t.sb("ffn_row", [P, D]), t.sb("fs", [P, N])
        tb, hb = t.ps("yT_banks", [P, 2, 512]), t.ps("h1_banks", [P, 4, 512])
        jobs = [(a, i) for a in range(NB) for i in range(N)]
        names = ("x_full", "yt_mm", "yt_s", "h_mm", "h_s", "sq_s", "root", "xn_s", "dch")
        s = {n: t.sem("d_" + n) for n in names}
        block = ctx.enter_context(nc.Block())

        @block.sync
        def _(sp):
            sp.dma_start(h1[:, xt[0]:xt[0] + N, :],
                         dram["x"][xt[0] * P:(xt[0] + N) * P, :].rearrange("(t p) d -> p t d", p=P)
                         ).then_inc(s["x_full"], 16)
            sp.dma_start(frow[:], rows(dram["ffn_norm"], P)).then_inc(s["x_full"], 16)
            W.load(sp, [(s["h_mm"], N * (a + 1)) for a in range(NB)])

        @block.gpsimd
        def _(pool):
            mix.pool(pool, sum(beats.values()))

        @block.tensor
        def _(pe):
            for m in range(2 * N):
                i, half = m // 2, m % 2
                if m >= 2:
                    pe.wait_ge(s["yt_s"], m - 1)
                for k in range(4):
                    tr = pe.transpose(tb[:, half, k * P:(k + 1) * P],
                                      y[:, xt[i], (4 * half + k) * P:(4 * half + k + 1) * P], ident[:])
                tr.then_inc(s["yt_mm"], 1)
            pe.wait_ge(s["yt_s"], 2 * N)
            for m, (a, i) in enumerate(jobs):
                if i == 0:
                    w = W.take(pe)
                if m >= 4:
                    pe.wait_ge(s["h_s"], m - 3)
                for k in range(KD):
                    mm = pe.matmul(hb[:, m % 4, 0:WCOLS], yT[:, i, k, :], w[:, k, :], start=(k == 0), stop=(k == KD - 1))
                mm.then_inc(s["h_mm"], 1)
                mix.pe(pe, pe_beats.get(m, 0))

        @block.scalar
        def _(act):
            for m in range(2 * N):
                i, half = m // 2, m % 2
                act.wait_ge(s["yt_mm"], m + 1)
                act.activation(yT[:, i, 4 * half:4 * half + 4, :], tb[:, half, :].rearrange("p (a b) -> p a b", a=4),
                               ACT.Copy).then_inc(s["yt_s"], 1)
            for m in range(len(jobs)):
                mix.act(act, act_beats.get(m, 0))
            for i in range(N):
                act.wait_ge(s["h_s"], len(jobs) - N + i + 1)
                act.activation(y[:, xt[i], :], h1[:, xt[i], :], ACT.Square, accum_out=fs[:, i:i + 1]
                               ).then_inc(s["sq_s"], 1)
                act.wait_ge(s["sq_s"], i + 1)
                act.activation(fs[:, i:i + 1], fs[:, i:i + 1], ACT.Sqrt, bias=cst["eps"][:],
                               scale=1.0 / D).then_inc(s["root"], 1)

        @block.vector
        def _(dve):
            link = chain(dve, s["dch"])
            dve.wait_ge(s["x_full"], 32)
            for m, (a, i) in enumerate(jobs):
                dve.wait_ge(s["h_mm"], m + 1)
                part_row = h1[:, xt[i], a * WCOLS:(a + 1) * WCOLS]
                dve.tensor_tensor(part_row, part_row, hb[:, m % 4, 0:WCOLS], ALU.add).then_inc(s["h_s"], 1)
                mix.dve(dve, beats.get(m, 0))
            for i in range(N):
                dve.wait_ge(s["root"], i + 1)
                link(dve.reciprocal(fs[:, i:i + 1], fs[:, i:i + 1]))
                dve.scalar_tensor_tensor(out=y[:, xt[i], :], in0=h1[:, xt[i], :], scalar=fs[:, i:i + 1], in1=frow[:],
                                         op0=ALU.mult, op1=ALU.mult).then_inc(s["xn_s"], 1)


def key_scores(nc, dram, cst, xn, scores, W, mix, part, beats):
    with ExitStack() as ctx:
        t = Tools(nc, ctx)
        act_beats, pe_beats = later(beats, 1), later(beats, 2)
        ident, HP = cst["ident"], 2 * H
        xt = [j - 1 for j in PARTS[part] if j]
        N = len(xt)
        keys, keysT = t.sb("keys", [P, HP, P]), t.sb("keysT", [P, HP, P])
        xnT, qT = t.sb("xnT", [P, KD, N * P]), t.sb("peer_qT", [P, 2, N * P])
        bank = t.ps("key_banks", [P, 6, 512])
        names = ("w_full", "k_full", "tr_mm", "tr_s", "q_mm", "q_s", "sc_mm", "sc_s")
        s = {n: t.sem("e_" + n) for n in names}
        turns = [(keysT[:, 4 * g:4 * g + 4, :], [keys[:, 4 * g + k, :] for k in range(4)]) for g in range(HP // 4)]
        turns += [(xnT[:, 4 * g:4 * g + 4, P * i:P * (i + 1)], [xn[:, xt[i], P * (4 * g + k):P * (4 * g + k + 1)] for k in range(4)])
                  for i in range(N) for g in range(2)]
        block = ctx.enter_context(nc.Block())

        @block.sync
        def _(sp):
            sp.dma_start(keys[:], dram["sub_keys"].rearrange("h s k c -> k (h s) c")).then_inc(s["k_full"], 16)
            W.load(sp, [(s["q_mm"], 2 * (a + 1)) for a in range(H)])

        @block.gpsimd
        def _(pool):
            mix.pool(pool, sum(beats.values()))

        @block.tensor
        def _(pe):
            pe.wait_ge(s["k_full"], 16)
            for m, (_, blocks) in enumerate(turns):
                if m >= 2:
                    pe.wait_ge(s["tr_s"], m - 1)
                for k, b in enumerate(blocks):
                    tr = pe.transpose(bank[:, m % 2, k * P:(k + 1) * P], b, ident[:])
                tr.then_inc(s["tr_mm"], 1)
            pe.wait_ge(s["tr_s"], len(turns))
            for i in range(HP + 1):
                if i < HP:
                    if i % 2 == 0:
                        w = W.take(pe)
                    if i >= 2:
                        pe.wait_ge(s["q_s"], i - 1)
                    for k in range(KD):
                        mm = pe.matmul(bank[:, 2 + i % 2, 0:N * P], w[:, k, (i % 2) * P:(i % 2 + 1) * P], xnT[:, k, :],
                                       start=(k == 0), stop=(k == KD - 1))
                    mm.then_inc(s["q_mm"], 1)
                if i:
                    j = i - 1
                    pe.wait_ge(s["q_s"], j + 1)
                    if j >= 2:
                        pe.wait_ge(s["sc_s"], j - 1)
                    for tt in range(N):
                        mm = pe.matmul(bank[:, 4 + j % 2, tt * P:(tt + 1) * P], qT[:, j % 2, tt * P:(tt + 1) * P],
                                       keysT[:, j, :], start=True, stop=True)
                    mm.then_inc(s["sc_mm"], 1)
                    mix.pe(pe, pe_beats.get(j, 0))

        @block.scalar
        def _(act):
            for i in range(HP):
                act.wait_ge(s["q_mm"], i + 1)
                if i >= 2:
                    act.wait_ge(s["sc_mm"], i - 1)
                act.activation(qT[:, i % 2, :], bank[:, 2 + i % 2, 0:N * P], ACT.Copy).then_inc(s["q_s"], 1)
                if i:
                    mix.act(act, act_beats.get(i - 1, 0))
            mix.act(act, act_beats.get(HP - 1, 0))

        @block.vector
        def _(dve):
            for m, (dst, _) in enumerate(turns):
                dve.wait_ge(s["tr_mm"], m + 1)
                dve.tensor_copy(dst, bank[:, m % 2, :].rearrange("p (a b) -> p a b", a=4)).then_inc(s["tr_s"], 1)
            for j in range(HP):
                dve.wait_ge(s["sc_mm"], j + 1)
                dve.tensor_copy(scores[:, :, j, :], bank[:, 4 + j % 2, 0:N * P].rearrange("p (a b) -> p a b", a=N)
                                ).then_inc(s["sc_s"], 1)
                mix.dve(dve, beats.get(j, 0))


def choose(nc, cst, scores, idx, gates, mix, tt, beats, first):
    with ExitStack() as ctx:
        t = Tools(nc, ctx)
        K, B = TOPK, 4
        LOW = -3.0e38
        left = t.sb("left", [P, B, KEYS])
        sv, si = t.sb("sv", [P, 2 * B, K]), t.sb("si", [P, 2 * B, K], U32)
        sif = t.sb("sif", [P, 2 * B, K])
        cand, cleft = t.sb("cand", [P, B, K, K]), t.sb("cleft", [P, B, K * K])
        cv, ci = t.sb("cv", [P, B, K]), t.sb("ci", [P, B, K], U32)
        ab, abf = t.sb("ab_i", [P, 2, B, K], U32), t.sb("ab_f", [P, 2, B, K])
        hot = t.sb("hot", [P, B * K, K])
        pick = t.sb("pick", [P, 2, B * K])
        gsum = t.sb("gsum", [P, B])
        dch, cv_s, exp_s, ready = t.sem("f_dch"), t.sem("f_cv"), t.sem("f_exp"), t.sem("f_ready")
        upto = lambda a, b: sum(beats.get(k, 0) for k in range(a, b))
        block = ctx.enter_context(nc.Block())

        @block.gpsimd
        def _(pool):
            if first:
                pool.wait_ge(ready, 1)
            mix.pool(pool, upto(0, 10))

        @block.tensor
        def _(pe):
            mix.pe(pe, upto(0, 10))

        @block.scalar
        def _(act):
            for g, (a, b) in enumerate(((0, 3), (3, 8))):
                mix.act(act, upto(a, b))
                gt = gates[:, tt * SLOTS + g * B * K:tt * SLOTS + (g + 1) * B * K]
                act.wait_ge(cv_s, g + 1)
                act.activation(gt, gt, ACT.Exp).then_inc(exp_s, 1)
                if first and g == 0:
                    act.wait_ge(ready, 1)
            mix.act(act, upto(8, 10))

        @block.vector
        def _(dve):
            link = chain(dve, dch)

            step = iter(range(1000))

            def beat():
                mix.dve(dve, beats.get(next(step), 0))

            def top16(srcs, lefts, vals, inds):
                n = len(srcs)
                for i in range(n):
                    ins = dve.max(vals[i][:, 0:8], srcs[i])
                link(ins)
                for i in range(n):
                    dve.max_index(inds[i][:, 0:8], vals[i][:, 0:8], srcs[i])
                    ins = dve.match_replace(lefts[i], vals[i][:, 0:8], srcs[i], LOW)
                link(ins)
                for i in range(n):
                    ins = dve.max(vals[i][:, 8:16], lefts[i])
                link(ins)
                for i in range(n):
                    ins = dve.max_index(inds[i][:, 8:16], vals[i][:, 8:16], lefts[i])
                link(ins)
                beat()

            for g in range(H // B):
                for b in range(0, 2 * B, B):
                    top16([scores[:, tt % 2, 2 * B * g + b + i, :] for i in range(B)], [left[:, i, :] for i in range(B)],
                          [sv[:, b + i, :] for i in range(B)], [si[:, b + i, :] for i in range(B)])
                dve.tensor_copy(sif[:], si[:])
                for i in range(B):
                    ins = dve.tensor_tensor(cand[:, i, :, :], sv[:, 2 * i, :].unsqueeze(2).to_broadcast([P, K, K]),
                                            sv[:, 2 * i + 1, :].unsqueeze(1).to_broadcast([P, K, K]), ALU.add)
                link(ins)
                top16([cand[:, i, :, :].rearrange("p a b -> p (a b)") for i in range(B)],
                      [cleft[:, i, :] for i in range(B)],
                      [cv[:, i, :] for i in range(B)], [ci[:, i, :] for i in range(B)])
                here = slice(tt * SLOTS + g * B * K, tt * SLOTS + (g + 1) * B * K)
                gt = gates[:, here].rearrange("p (h k) -> p h k", h=B)
                dve.tensor_tensor(gt, cv[:], cv[:, :, 0:1].to_broadcast([P, B, K]), ALU.subtract).then_inc(cv_s, 1)
                dve.tensor_scalar(ab[:, 0, :, :], ci[:], 4, None, ALU.logical_shift_right)
                link(dve.tensor_scalar(ab[:, 1, :, :], ci[:], 15, None, ALU.bitwise_and))
                link(dve.tensor_copy(abf[:], ab[:]))
                for o in range(2):
                    link(dve.tensor_tensor(hot[:], abf[:, o, :, :].rearrange("p h k -> p (h k)").unsqueeze(2)
                                           .to_broadcast([P, B * K, K]),
                                           cst["iota16"][:].unsqueeze(1).to_broadcast([P, B * K, K]), ALU.is_equal))
                    hv = hot[:].rearrange("p (h k) a -> p h k a", h=B)
                    link(dve.tensor_tensor(hv, hv, sif[:, o::2, :].unsqueeze(2).to_broadcast([P, B, K, K]), ALU.mult))
                    link(dve.tensor_reduce(pick[:, o, :], hot[:], AX, ALU.add))
                    if o == 0:
                        beat()
                link(dve.scalar_tensor_tensor(out=idx[:, here], in0=pick[:, 0, :], scalar=float(KEYS),
                                              in1=pick[:, 1, :], op0=ALU.mult, op1=ALU.add))
                dve.wait_ge(exp_s, g + 1)
                link(dve.tensor_reduce(gsum[:], gt, AX, ALU.add))
                link(dve.reciprocal(gsum[:], gsum[:]))
                dve.tensor_tensor(gt, gt, gsum[:].unsqueeze(2).to_broadcast([P, B, K]), ALU.mult).then_inc(ready, 1)
                dve.wait_ge(ready, g + 1)
                beat()


def mix_rest(nc, dram, cst, mix, xn, h1, idx, gates, acc, out):
    with ExitStack() as ctx:
        t = Tools(nc, ctx)
        ident, done = cst["ident"], mix.at["pe"]
        assert done % BIG == 0 and set(mix.at.values()) == {done}
        stage = t.sb("stage", [P, 2, BIG], I32)
        uring, vring = t.sb("big_uring", [P, BIG, D]), t.sb("big_vring", [P, BIG, D])
        dots, acts, weights = (t.sb("big_" + n, [P, BIG]) for n in ("dots", "acts", "weights"))
        diag = t.sb("big_diag", [P, BIG, P])
        u_full = [t.sem(f"big_u_full{i}") for i in range(BIG)]
        v_full = [t.sem(f"big_v_full{i}") for i in range(BIG)]
        staged, issued, dotted, gelued = t.sem("staged"), t.sem("issued"), t.sem("big_dotted"), t.sem("big_gelued")
        weighted, diag_s, combined = t.sem("weighted"), t.sem("big_diag_s"), t.sem("big_combined")
        rows_out, stored = mix.rows_out, mix.stored
        first, last = done // BIG, XT * SLOTS // BIG
        per = SLOTS // BIG
        spans = [(max(first, tt * per), (tt + 1) * per, tt) for tt in range(XT) if (tt + 1) * per > first]
        block = ctx.enter_context(nc.Block())

        @block.sync
        def _(sp):
            for tt in range(XT):
                sp.wait_ge(rows_out, tt + 1)
                sp.dma_start(out[0, tt * P:(tt + 1) * P, :], h1[:, tt, :]).then_inc(stored, 16)
            sp.wait_ge(stored, 16 * XT)

        @block.gpsimd
        def _(pool):
            def group(count, at, hf):
                pool.tensor_copy(stage[:, hf, :], idx[:, at]).then_inc(staged, 1)
                pool.wait_ge(staged, count + 1)
                for k in range(BIG):
                    row = bass.IndirectOffsetOnAxis(ap=stage[:, hf, k:k + 1].bitcast(U32), axis=0)
                    pool.wait_ge(dotted, count * BIG + (k + 1))
                    pool.sem_inc(issued, 1)
                    pool.indirect_dma_start(uring[:, k, :], None, dram["expert_u"], row).then_inc(u_full[k], 16)
                    pool.wait_ge(combined, count * BIG + (k + 1))
                    pool.sem_inc(issued, 1)
                    pool.indirect_dma_start(vring[:, k, :], None, dram["expert_v"], row).then_inc(v_full[k], 16)

            pairs = (last - first) // 2
            with pool.Fori(0, pairs) as i:
                for hf in range(2):
                    group(i * 2 + hf, bass.ds(i * (2 * BIG) + (done + hf * BIG), BIG), hf)
            if (last - first) % 2:
                group(2 * pairs, slice(done + 2 * pairs * BIG, done + (2 * pairs + 1) * BIG), 0)

        @block.vector
        def _(dve):
            dve.sem_inc(dotted, BIG)
            if done % SLOTS == 0:
                mix.finish_tile(dve, done // SLOTS - 1)
            for a, b, tt in spans:
                with dve.Fori(a - first, b - first) as g:
                    for k in range(BIG):
                        dve.wait_ge(u_full[k], (g + 1) * 16)
                        dve.tensor_tensor_reduce(out=uring[:, k, :], in0=uring[:, k, :], in1=xn[:, tt, :], scale=1.0,
                                                 scalar=0.0, op0=ALU.mult, op1=ALU.add,
                                                 accum_out=dots[:, k:k + 1]).then_inc(dotted, 1)
                        if k % BIGHALF == BIGHALF - 1:
                            c = k + 1 - BIGHALF
                            dve.wait_ge(gelued, g * 2 + (k // BIGHALF + 1))
                            dve.tensor_tensor(weights[:, c:c + BIGHALF], acts[:, c:c + BIGHALF],
                                              gates[:, bass.ds(g * BIG + (done + c), BIGHALF)], ALU.mult
                                              ).then_inc(weighted, 1)
                dve.wait_ge(combined, BIG + BIG * (b - first))
                dve.tensor_copy(h1[:, tt, :], acc[:]).then_inc(rows_out, 1)

        @block.scalar
        def _(act):
            with act.Fori(0, last - first) as g:
                for hf in range(BIG // BIGHALF):
                    b = hf * BIGHALF
                    act.wait_ge(dotted, g * BIG + (b + BIGHALF + BIG))
                    act.activation(acts[:, b:b + BIGHALF], dots[:, b:b + BIGHALF], ACT.Gelu).then_inc(gelued, 1)
                    act.wait_ge(weighted, g * 2 + (hf + 1))
                    act.wait_ge(combined, g * BIG + (b + BIGHALF))
                    for k in range(b, b + BIGHALF):
                        act.activation(diag[:, k, :], ident[:], ACT.Copy, scale=weights[:, k:k + 1]).then_inc(diag_s, 1)

        @block.tensor
        def _(pe):
            pe.sem_inc(combined, BIG)
            for a, b, tt in spans:
                if a == tt * per:
                    mix.seed(pe, tt)
                with pe.Fori(a - first, b - first) as g:
                    for k in range(BIG):
                        pe.wait_ge(v_full[k], (g + 1) * 16)
                        pe.wait_ge(diag_s, g * BIG + (k + 1))
                        for n in range(2):
                            mm = pe.matmul(acc[:, n * 512:(n + 1) * 512], diag[:, k, :],
                                           vring[:, k, n * 512:(n + 1) * 512],
                                           start=False, stop=False, skip_group_check=True)
                        mm.then_inc(combined, 1)


def constants():
    i = np.arange(P)
    a, b = i[:, None], i[None, :]
    levels = np.zeros((P, LEVELS, P), np.float32)
    for l in range(LEVELS):
        s = 1 << l
        levels[:, l, :] = (a // (2 * s) == b // (2 * s)) & (a % (2 * s) < s) & (b % (2 * s) >= s)
    half = ROPE // 2
    inv = np.exp((-np.log(10000.0) * np.arange(half, dtype=np.float32) * np.float32(2.0 / ROPE)).astype(np.float32))
    ang = np.arange(T, dtype=np.float32)[:, None] * inv[None, :].astype(np.float32)

    def by_tile(x):
        out = np.zeros((P, NT, half), np.float32)
        for j in range(NT):
            out[0:SIZE[j], j] = x[START[j]:START[j] + SIZE[j]]
        return out
    return {
        "ident": np.eye(P, dtype=np.float32),
        "triu": (a <= b).astype(np.float32),
        "maskT": np.where(a <= b, 0.0, NEG).astype(np.float32),
        "mask": np.where(a >= b, 0.0, NEG).astype(np.float32),
        "levels": levels,
        "pair_ones": (a // DK == b // DK).astype(np.float32),
        "cos": by_tile(np.cos(ang).astype(np.float32)),
        "sin": by_tile(np.sin(ang).astype(np.float32)),
        "iota16": np.tile(np.arange(TOPK, dtype=np.float32), (P, 1)),
    }


def spread(keys, n):
    out, given = {}, 0
    for i, k in enumerate(keys):
        out[k] = (n * (i + 1) // len(keys)) // PAIR * PAIR - given
        given += out[k]
    return out


def later(beats, n):
    keys = list(beats)
    out = {k: beats[keys[i - n]] if i >= n else 0 for i, k in enumerate(keys)}
    if keys:
        out[keys[-1]] += sum(beats[k] for k in keys[-n:])
    return out


def layer(nc, dram, out, shapes):
    with ExitStack() as ctx:
        t = Tools(nc, ctx)
        cst = {name: t.sb("k_" + name, list(shape)) for name, shape in shapes.items()}
        cst["eps"] = t.sb("k_eps", [P, 1])
        cst["loaded"], cst["eps_set"] = t.sem("consts_loaded"), t.sem("eps_set")
        y, h1 = t.sb("y", [P, XT, D]), t.sb("h1", [P, XT, D])
        idx, gates = t.sb("idx", [P, XT * SLOTS], I32), t.sb("gates", [P, XT * SLOTS])
        acc = t.ps("acc", [P, D])
        with ExitStack() as front:
            f = Tools(nc, front)
            W = Weights(f, dram)
            mix = Mixing(nc, t, f, dram, cst, y, h1, idx, gates, acc, out)
            state = {"hist": f.sb("hist", [P, QC, CONV - 1]), "cw": f.sb("conv_cols", [P, QC * CONV]),
                     "S": f.sb("S", [P, 4, DK]), "kT": f.sb("kT", [QKD, H, T]), "V": f.sb("V", [P, NT, H, 64]), "y": y}
            for part in range(len(PARTS)):
                NJ = len(PARTS[part])
                n = SHARE if part else dict.fromkeys(SHARE, 0)
                with ExitStack() as tokens:
                    m = Tools(nc, tokens)
                    keep = dict(state, rest=m.sb("rest", [P, NJ, REST]))
                    with ExitStack() as conv:
                        TP = sum(SIZE[j] for j in PARTS[part])
                        keep["sT"] = Tools(nc, conv).sb("sT", [P, QC, TP])
                        project(nc, dram, cst, keep, W, mix, part, spread(list(range(QC + 8)), n["project"]))
                        steps = [("n", c) for c in range(8)] if part else []
                        for jj in range(NJ):
                            steps += [("g", jj), ("a", jj)] + [("l", jj, l) for l in range(1, LEVELS)] + [("w", jj), ("o", jj)]
                        delta_rule(nc, dram, cst, keep, mix, part, spread(steps, n["delta_rule"]))
                    steps = [("t", jj) for jj in range(NJ) for _ in range(1)] + [("u", i) for i in range(2 * H)]
                    latent_attention(nc, dram, cst, keep, mix, part, spread(steps, n["attention"]))
                out_project(nc, dram, cst, y, h1, W, mix, part, spread(list(range(8)), n["out_project"]))
                with ExitStack() as sel:
                    scores = Tools(nc, sel).sb("scores", [P, 2, 2 * H, KEYS])
                    key_scores(nc, dram, cst, y, scores, W, mix, part, spread(list(range(2 * H)), n["key_scores"]))
                    for i, steps, k in ((0, list(range(6, 10)), "choose_own"), (1, list(range(10)), "choose_second")
                                        ) if part == 0 else ((0, list(range(10)), "choose_first"),
                                                             (1, list(range(10)), "choose_second")):
                        choose(nc, cst, scores, idx, gates, mix, 2 * part + i, spread(steps, SHARE[k]), k == "choose_own")
        mix_rest(nc, dram, cst, mix, y, h1, idx, gates, acc, out)


_PLAIN = ["w_in", "conv_w", "w_uq", "w_ukv", "w_out", "w_pq", "expert_u", "expert_v"]
_VECTORS = ["attn_norm", "a_log", "dt_bias", "gdn_norm", "q_a_norm", "kv_a_norm", "q_norm", "k_norm", "ffn_norm"]


def kernel(**inputs):
    import numpy as _np
    import concourse.bacc as _bacc
    from concourse import mybir as _mybir
    from concourse.bass_utils import run_bass_kernel_spmd as _run

    arrays = {"x": inputs["x"][0], "meta": inputs["meta_tokens"], "sub_keys": inputs["sub_keys"][0]}
    for name in _PLAIN + _VECTORS:
        arrays[name] = inputs[name][0]
    consts = constants()
    for name, a in consts.items():
        arrays["c_" + name] = a
    arrays = {name: _np.ascontiguousarray(a) for name, a in arrays.items()}
    nc = _bacc.Bacc("TRN2", target_bir_lowering=False, num_devices=1)
    dram = {name: nc.dram_tensor(f"in_{name}", a.shape, _mybir.dt.from_np(a.dtype), kind="ExternalInput").ap()
            for name, a in arrays.items()}
    out = nc.dram_tensor("out_0", (1, SEQ, D), _mybir.dt.float32, kind="ExternalOutput").ap()
    layer(nc, dram, out, {name: a.shape for name, a in consts.items()})
    r = _run(nc, [{f"in_{name}": a for name, a in arrays.items()}], core_ids=[0])
    return r.results[0]["out_0"]
```

```python
from contextlib import ExitStack

import numpy as np

import concourse.bass as bass
from concourse import mybir

F32 = mybir.dt.float32
I32 = mybir.dt.int32
U32 = mybir.dt.uint32
ALU = mybir.AluOpType
ACT = mybir.ActivationFunctionType
AX = mybir.AxisListType.X

P = 128
D = 1024
SEQ = 512
META = 16
T = META + SEQ
KD = D // P
EPS = 1e-6
NEG = -1e30
H = 8
DK = 64
CONV = 4
QKV = 3 * H * DK
QC = QKV // P
REST = 944
Z0, B0, A0, CQ0, CKV0, KPE0 = 0, 512, 520, 528, 784, 912
QL, KL, NOPE, ROPE, QKD = 256, 128, 64, 32, 96
SCALE = QKD ** -0.5
LEVELS = 7
TOPK = 16
KEYS = 128
SLOTS = H * TOPK
XT = SEQ // P
SIZE = [META] + [P] * XT
START = [0] + [META + P * t for t in range(XT)]
NT = len(SIZE)
PARTS = [[0, 1, 2], [3, 4]]
WCOLS = 256
URING, DRING, RING, PAIR = 4, 4, 8, 2
AHEAD = 2
BIG, BIGHALF = 8, 4


def chain(eng, sem):
    def link(ins):
        link.count += 1
        ins.then_inc(sem, 1)
        eng.wait_ge(sem, link.count)
    link.count = 0
    return link


class Tools:
    taken = {}

    def __init__(self, nc, ctx):
        self.nc, self.ctx, self.sems = nc, ctx, []
        ctx.callback(self.close)

    def close(self):
        if self.sems:
            self.nc.clear_and_free_semaphores(self.sems)
            self.nc.all_engine_barrier()

    def unique(self, name):
        n = self.taken[self.nc, name] = self.taken.get((self.nc, name), 0) + 1
        return name if n == 1 else f"{name}_{n}"

    def sb(self, name, shape, dt=F32):
        return self.ctx.enter_context(self.nc.sbuf_tensor(self.unique(name), shape, dt))

    def ps(self, name, shape, dt=F32):
        return self.ctx.enter_context(self.nc.psum_tensor(self.unique(name), shape, dt))

    def sem(self, name):
        self.sems.append(self.nc.alloc_semaphore(name=self.unique(name)))
        return self.sems[-1]


class Weights:
    def __init__(self, t, dram):
        self.buf = t.sb("w_blocks", [P, 2, KD, WCOLS])
        self.full = [t.sem("w_full0"), t.sem("w_full1")]
        self.plan = []
        for _ in PARTS:
            for name, width in (("w_in", QKV + REST), ("w_out", D), ("w_pq", 2 * H * P)):
                w = dram[name].rearrange("(k p) n -> p k n", p=P)
                self.plan += [w[:, :, a:min(a + WCOLS, width)] for a in range(0, width, WCOLS)]
        self.loaded = self.loaded_by_phase = self.taken = 0

    def load(self, sp, ends):
        first, last = self.loaded_by_phase, self.loaded_by_phase + len(ends)
        while self.loaded < min(last + 2, len(self.plan)):
            n, src = self.loaded, self.plan[self.loaded]
            if n - 2 >= first:
                sp.wait_ge(*ends[n - 2 - first])
            sp.dma_start(self.buf[:, n % 2, :, 0:src.shape[2]], src).then_inc(self.full[n % 2], 16)
            self.loaded += 1
        self.loaded_by_phase = last

    def take(self, pe):
        n = self.taken
        self.taken += 1
        pe.wait_ge(self.full[n % 2], 16 * (n // 2 + 1))
        return self.buf[:, n % 2, :, :]


class Mixing:
    def __init__(self, nc, whole, t, dram, cst, xn, h1, idx, gates, acc, out, total):
        self.ident, self.xn, self.h1, self.idx, self.gates = cst["ident"], xn, h1, idx, gates
        self.acc, self.out, self.u, self.v = acc, out, dram["expert_u"], dram["expert_v"]
        self.uring, self.vring = t.sb("uring", [P, URING, D]), t.sb("vring", [P, RING, D])
        self.dots, self.acts = t.sb("dots", [P, RING]), t.sb("acts", [P, RING])
        self.weights, self.diag = t.sb("weights", [P, RING]), t.sb("diag", [P, DRING, P])
        self.u_full = [whole.sem(f"u_full{i}") for i in range(URING)]
        self.v_full = [whole.sem(f"v_full{i}") for i in range(RING)]
        self.dotted, self.gelued, self.scaled = whole.sem("dotted"), whole.sem("gelued"), whole.sem("scaled")
        self.diag_s, self.combined = whole.sem("diag_s"), whole.sem("combined")
        self.rows_out, self.stored = whole.sem("rows_out"), whole.sem("stored")
        self.at = {"pool": 0, "dve": 0, "act": 0, "pe": 0}
        self.total, self.granted, self.over = total, 0, {1: [0], 2: [0, 0]}

    def _next(self, engine, n):
        a = self.at[engine]
        self.at[engine] = a + n
        return range(a, a + n)

    def later(self, beats, lag):
        line = self.over[lag] + list(beats.values())
        self.over[lag] = line[len(beats):]
        return dict(zip(beats, line))

    def leftover(self, lag):
        n, self.over[lag] = sum(self.over[lag]), [0] * lag
        return n

    def pool(self, pool, n):
        if n == 0:
            return
        self.granted += n
        for i in self._next("pool", min(self.granted + AHEAD, self.total) - self.at["pool"]):
            k, ku = i % RING, i % URING
            row = bass.IndirectOffsetOnAxis(ap=self.idx[:, i:i + 1].bitcast(U32), axis=0)
            if i >= URING:
                pool.wait_ge(self.dotted, i - URING + 1)
            pool.indirect_dma_start(self.uring[:, ku, :], None, self.u, row).then_inc(self.u_full[ku], 16)
            if i >= RING:
                pool.wait_ge(self.combined, i - RING + 1)
            pool.indirect_dma_start(self.vring[:, k, :], None, self.v, row).then_inc(self.v_full[k], 16)

    def dve(self, dve, n):
        for i in self._next("dve", n):
            k, ku, tt = i % RING, i % URING, i // SLOTS
            if i and i % SLOTS == 0:
                self.finish_tile(dve, tt - 1)
            dve.wait_ge(self.u_full[ku], 16 * (i // URING + 1))
            if i >= RING:
                dve.wait_ge(self.gelued, (i - RING) // PAIR + 1)
            dve.tensor_tensor_reduce(out=self.uring[:, ku, :], in0=self.uring[:, ku, :], in1=self.xn[:, tt, :],
                                     scale=1.0, scalar=0.0, op0=ALU.mult, op1=ALU.add,
                                     accum_out=self.dots[:, k:k + 1]).then_inc(self.dotted, 1)

    def finish_tile(self, dve, tt):
        dve.wait_ge(self.combined, SLOTS * (tt + 1))
        dve.tensor_copy(self.h1[:, tt, :], self.acc[:]).then_inc(self.rows_out, 1)

    def act(self, act, n):
        assert n % PAIR == 0
        for i in self._next("act", n)[::PAIR]:
            b, bd = i % RING, i % DRING
            act.wait_ge(self.dotted, i + PAIR)
            if i >= DRING:
                act.wait_ge(self.combined, i - DRING + PAIR)
            act.activation(self.acts[:, b:b + PAIR], self.dots[:, b:b + PAIR], ACT.Gelu).then_inc(self.gelued, 1)
            act.wait_ge(self.gelued, i // PAIR + 1)
            for m in range(PAIR):
                act.activation(self.weights[:, b + m:b + m + 1], self.acts[:, b + m:b + m + 1], ACT.Copy,
                               scale=self.gates[:, i + m:i + m + 1]).then_inc(self.scaled, 1)
            act.wait_ge(self.scaled, i + PAIR)
            for m in range(PAIR):
                act.activation(self.diag[:, bd + m, :], self.ident[:], ACT.Copy,
                               scale=self.weights[:, b + m:b + m + 1]).then_inc(self.diag_s, 1)

    def pe(self, pe, n):
        for i in self._next("pe", n):
            k, tt = i % RING, i // SLOTS
            if i % SLOTS == 0:
                self.seed(pe, tt)
            pe.wait_ge(self.v_full[k], 16 * (i // RING + 1))
            pe.wait_ge(self.diag_s, i + 1)
            for a in range(2):
                mm = pe.matmul(self.acc[:, a * 512:(a + 1) * 512], self.diag[:, i % DRING, :],
                               self.vring[:, k, a * 512:(a + 1) * 512], start=False, stop=False, skip_group_check=True)
            mm.then_inc(self.combined, 1)

    def seed(self, pe, tt):
        if tt:
            pe.wait_ge(self.rows_out, tt)
        for a in range(2):
            mm = pe.matmul(self.acc[:, a * 512:(a + 1) * 512], self.ident[:], self.h1[:, tt, a * 512:(a + 1) * 512],
                           start=True, stop=False, skip_group_check=True)


def rows(ap, n):
    return bass.AP(tensor=ap.tensor, offset=ap.offset, ap=[[0, n]] + [list(x) for x in ap.ap])
SHARE = {"project": 34, "delta_rule": 60, "attention": 44, "out_project": 16, "score_and_choose": 40,
         "score_own": 14, "choose": 32}


def project(nc, dram, cst, keep, W, mix, part, beats):
    with ExitStack() as ctx:
        t = Tools(nc, ctx)
        act_beats, pe_beats = mix.later(beats, 1), mix.later(beats, 2)
        tiles = PARTS[part]
        NJ, t0 = len(tiles), START[tiles[0]]
        TP = sum(SIZE[j] for j in tiles)
        hx, hs = t.sb("hx", [P, NJ, D]), t.sb("hs", [P, 2, D])
        arow = t.sb("attn_norm_row", [P, D])
        hnT = t.sb("hnT", [P, KD, TP])
        raw = t.sb("raw", [P, 2, CONV - 1 + TP])
        ss, rs = t.sb("ss", [P, NJ]), t.sb("rs", [P, NJ])
        cw4 = t.sb("conv_rows", [CONV, QKV]) if part == 0 else None
        tp, pp = t.ps("turn_banks", [P, 2, 512]), t.ps("project_banks", [P, 4, 512])
        names = ("x_in0", "x_in1", "x_in2", "row_in", "cw_in", "squared", "rooted", "normed", "turned", "hnT_s", "cw_mm", "cw_s",
                 "proj", "raw_s", "tail_s", "conved", "silued", "rest_mm", "rest_s", "dch", "init")
        s = {n: t.sem("a_" + n) for n in names}
        ident, sT, rest, hist, cw = cst["ident"], keep["sT"], keep["rest"], keep["hist"], keep["cw"]
        NB = (REST + WCOLS - 1) // WCOLS
        OTHERS = ("triu", "maskT", "mask", "levels", "norm_sum", "cos", "sin", "iota16")
        jobs = [(a, jj) for a in range(NB) for jj in range(NJ) if tiles[jj] or a * WCOLS >= B0]
        block = ctx.enter_context(nc.Block())

        @block.sync
        def _(sp):
            if part == 0:
                sp.dma_start(cst["ident"][:], dram["c_ident"]).then_inc(cst["ident_loaded"], 16)
            for jj, j in enumerate(tiles):
                src = dram["meta"] if j == 0 else dram["x"][(j - 1) * P:j * P, :]
                sp.dma_start(hx[0:SIZE[j], jj, :], src).then_inc(s[f"x_in{jj}"], 16)
                if jj == 0:
                    sp.dma_start(arow[:], rows(dram["attn_norm"], P)).then_inc(s["row_in"], 16)
            if part == 0:
                sp.dma_start(cw4[:], dram["conv_w"]).then_inc(s["cw_in"], 16)
            ends = [(s["proj"], c + 2) for c in range(0, QC, 2)]
            ends += [(s["rest_mm"], sum(1 for b, _ in jobs if b <= a)) for a in range(NB)]
            W.load(sp, ends)

        @block.gpsimd
        def _(pool):
            mix.pool(pool, sum(beats.values()))

        @block.scalar
        def _(act):
            for jj, j in enumerate(tiles):
                n = SIZE[j]
                act.wait_ge(s[f"x_in{jj}"], 16)
                if jj >= 2:
                    act.wait_ge(s["turned"], 2 * (jj - 1))
                act.activation(hs[0:n, jj % 2, :], hx[0:n, jj, :], ACT.Square,
                               accum_out=ss[0:n, jj:jj + 1]).then_inc(s["squared"], 1)
                act.wait_ge(s["squared"], jj + 1)
                if jj == 0 and part == 0:
                    act.wait_ge(cst["eps_set"], 1)
                act.activation(ss[0:n, jj:jj + 1], ss[0:n, jj:jj + 1], ACT.Sqrt, bias=cst["eps"][0:n, :],
                               scale=1.0 / D).then_inc(s["rooted"], 1)
            if part == 0:
                for name in OTHERS:
                    act.dma_start(cst[name][:], dram["c_" + name]).then_inc(cst["loaded"], 16)
                act.wait_ge(s["init"], 1)
            for c in range(QC):
                act.wait_ge(s["proj"], c + 1)
                if c >= 2:
                    act.wait_ge(s["conved"], c - 1)
                act.activation(raw[:, c % 2, 0:CONV - 1], hist[:, c, :], ACT.Copy).then_inc(s["raw_s"], 1)
                act.activation(raw[:, c % 2, CONV - 1:], pp[:, c % 4, 0:TP], ACT.Copy).then_inc(s["raw_s"], 1)
                if c:
                    act.wait_ge(s["conved"], c)
                    act.activation(sT[:, c - 1, 0:TP], sT[:, c - 1, 0:TP], ACT.Silu).then_inc(s["silued"], 1)
                act.wait_ge(s["raw_s"], 2 * c + 2)
                act.activation(hist[:, c, :], raw[:, c % 2, TP:TP + CONV - 1], ACT.Copy).then_inc(s["tail_s"], 1)
                mix.act(act, act_beats.get(c, 0))
            act.wait_ge(s["conved"], QC)
            act.activation(sT[:, QC - 1, 0:TP], sT[:, QC - 1, 0:TP], ACT.Silu).then_inc(s["silued"], 1)
            for m in range(len(jobs)):
                mix.act(act, act_beats.get(QC + m, 0))
            act.wait_ge(s["silued"], QC)
            act.wait_ge(s["tail_s"], QC)

        @block.vector
        def _(dve):
            link = chain(dve, s["dch"])
            if part == 0:
                dve.memset(cst["eps"][:], EPS).then_inc(cst["eps_set"], 1)
                dve.memset(hist[:], 0.0).then_inc(s["init"], 1)
                link(dve.memset(rest[:, 0, :], 0.0))
            dve.wait_ge(s["row_in"], 16)

            def norm(jj):
                n = SIZE[tiles[jj]]
                dve.wait_ge(s["rooted"], jj + 1)
                link(dve.reciprocal(rs[0:n, jj:jj + 1], ss[0:n, jj:jj + 1]))
                dve.scalar_tensor_tensor(out=hs[0:n, jj % 2, :], in0=hx[0:n, jj, :], scalar=rs[0:n, jj:jj + 1],
                                         in1=arow[0:n, :], op0=ALU.mult, op1=ALU.mult).then_inc(s["normed"], 1)

            norm(0)
            for jj, j in enumerate(tiles):
                if jj + 1 < NJ:
                    norm(jj + 1)
                for half in range(2):
                    dve.wait_ge(s["turned"], 2 * jj + half + 1)
                    dve.tensor_copy(hnT[:, 4 * half:4 * half + 4, START[j] - t0:START[j] - t0 + SIZE[j]],
                                    tp[:, half, :].rearrange("p (a b) -> p a b", a=4)[:, :, 0:SIZE[j]]
                                    ).then_inc(s["hnT_s"], 1)
            if part == 0:
                dve.wait_ge(s["cw_mm"], 1)
                dve.tensor_copy(cw[:], tp[:, 0, 0:QC * CONV]).then_inc(s["cw_s"], 1)
                dve.wait_ge(s["cw_s"], 1)
            for c in range(QC):
                dve.wait_ge(s["raw_s"], 2 * c + 2)
                for i in range(CONV):
                    src = raw[:, c % 2, i:i + TP]
                    tap = cw[:, c * CONV + i:c * CONV + i + 1]
                    if i == 0:
                        link(dve.tensor_scalar(sT[:, c, 0:TP], src, tap, None, ALU.mult))
                    else:
                        ins = dve.scalar_tensor_tensor(out=sT[:, c, 0:TP], in0=src, scalar=tap, in1=sT[:, c, 0:TP],
                                                       op0=ALU.mult, op1=ALU.add)
                        if i < CONV - 1:
                            link(ins)
                ins.then_inc(s["conved"], 1)
                mix.dve(dve, beats.get(c, 0))
            for m, (a, jj) in enumerate(jobs):
                dve.wait_ge(s["rest_mm"], m + 1)
                n, width = SIZE[tiles[jj]], min(WCOLS, REST - a * WCOLS)
                dve.tensor_copy(rest[0:n, jj, a * WCOLS:a * WCOLS + width], pp[0:n, m % 4, 0:width]
                                ).then_inc(s["rest_s"], 1)
                mix.dve(dve, beats.get(QC + m, 0))
            dve.wait_ge(s["rest_s"], len(jobs))

        @block.tensor
        def _(pe):
            if part == 0:
                pe.wait_ge(cst["ident_loaded"], 16)
            for jj, j in enumerate(tiles):
                n = SIZE[j]
                pe.wait_ge(s["normed"], jj + 1)
                for half in range(2):
                    if jj:
                        pe.wait_ge(s["hnT_s"], 2 * jj - 1 + half)
                    for k in range(4):
                        kk = 4 * half + k
                        tr = pe.transpose(tp[:, half, k * P:k * P + n], hs[0:n, jj % 2, kk * P:(kk + 1) * P],
                                          ident[0:n, 0:n])
                    tr.then_inc(s["turned"], 1)
            pe.wait_ge(s["hnT_s"], 2 * NJ)
            if part == 0:
                pe.wait_ge(s["cw_in"], 16)
                for c in range(QC):
                    tr = pe.transpose(tp[:, 0, c * CONV:(c + 1) * CONV], cw4[:, c * P:(c + 1) * P],
                                      ident[0:CONV, 0:CONV])
                tr.then_inc(s["cw_mm"], 1)
            for c in range(QC):
                if c % 2 == 0:
                    w = W.take(pe)
                if c >= 4:
                    pe.wait_ge(s["raw_s"], 2 * (c - 3))
                for k in range(KD):
                    mm = pe.matmul(pp[:, c % 4, 0:TP], w[:, k, (c % 2) * P:(c % 2 + 1) * P], hnT[:, k, :],
                                   start=(k == 0), stop=(k == KD - 1))
                mm.then_inc(s["proj"], 1)
                mix.pe(pe, pe_beats.get(c, 0))
            pe.wait_ge(s["raw_s"], 2 * QC)
            if part == 0:
                pe.wait_ge(cst["loaded"], 16 * len(OTHERS))
            for m, (a, jj) in enumerate(jobs):
                n, width, lo = SIZE[tiles[jj]], min(WCOLS, REST - a * WCOLS), START[tiles[jj]] - t0
                if m == 0 or jobs[m - 1][0] != a:
                    w = W.take(pe)
                if m >= 4:
                    pe.wait_ge(s["rest_s"], m - 3)
                for k in range(KD):
                    mm = pe.matmul(pp[0:n, m % 4, 0:width], hnT[:, k, lo:lo + n], w[:, k, 0:width],
                                   start=(k == 0), stop=(k == KD - 1))
                mm.then_inc(s["rest_mm"], 1)
                mix.pe(pe, pe_beats.get(QC + m, 0))


def delta_rule(nc, dram, cst, keep, mix, part, beats):
    with ExitStack() as ctx:
        t = Tools(nc, ctx)
        act_beats, pe_beats = mix.later(beats, 1), mix.later(beats, 2)
        sT, rest, y = keep["sT"], keep["rest"], keep["y"]
        ident, triu, maskT = cst["ident"], cst["triu"], cst["maskT"]
        levels, norm_sum = cst["levels"], cst["norm_sum"]
        HD = H * DK
        tiles = PARTS[part]
        NJ, t0 = len(tiles), START[tiles[0]]
        TP = sum(SIZE[j] for j in tiles)
        S = keep["S"]
        dtb, alog, grow = t.sb("dtb", [P, H]), t.sb("alog", [P, H]), t.sb("gdn_norm_row", [P, DK])
        xs, ab, e1, u1, l1, g, beta, gc, eg, kds, glE = (t.sb(n, [P, NJ, H]) for n in (
            "xs", "ab", "e1", "u1", "l1", "g", "beta", "gc", "eg", "kds", "glE"))
        glp, bg, orm = t.sb("glp", [P, 4]), t.sb("bg", [P, H]), t.sb("orm", [P, H])
        ones = t.sb("ones", [P, P])
        b1, b2, b3, b4, PT, X, XTr = (t.sb(n, [P, H, P]) for n in ("b1", "b2", "b3", "b4", "PT", "X", "XT"))
        gB, egB, Y = b1, b1, b1
        bB, BT1 = b2, b2
        decT, BT0 = b3, b3
        MT = b4
        sq = b1[:].rearrange("p h i -> p (h i)")[:, 0:2 * TP].rearrange("p (a i) -> p a i", a=2)
        norm_spread = b3[0:2 * 8, :, :]
        root = b2[0:2 * 8, :, :].rearrange("p h i -> p (h i)")[:, 0:TP]
        ktok, vtok = (X[:].rearrange("p h i -> p (h i)")[:, a * HD:(a + 1) * HD] for a in range(2))
        vb, kbg, kd, u, vn = (t.sb(n, [P, HD]) for n in ("vb", "kbg", "kd", "u", "vn"))
        osq, zs = u, vb
        wT, qgT = t.sb("wT", [P, 4, P]), t.sb("qgT", [P, 4, P])
        bank = t.ps("banks", [P, 6, 512])

        def quad(b, n):
            return bank[0:n, b, :].rearrange("p (h i) -> p h i", h=4)

        ORDER = [2 * i + o for o in range(2) for i in range(4)]

        def parity(ap, o):
            return ap.rearrange("p (c o d) -> p o c d", o=2, d=DK)[:, o, :, :]


        names = ("spread_in", "inverted", "norm_mm", "sqd", "normsum", "rooted", "qk_scaled", "turned", "turned_out", "vec_in", "beta_s", "exp_neg",
                 "abs_s", "ln_s", "alog_s", "g_s", "gb_s", "gates_mm", "gc_s", "bcast_mm", "dec_s", "eg_s", "egb_s",
                 "dec_exp", "kk_mm", "mt_s", "qk_mm", "pt_s", "sides_s", "bt_s", "y_mm", "y_out", "xy_mm", "x_s",
                 "uw_mm", "uw_s", "ws_mm", "qs_mm", "vn_s", "o_mm", "s_mm", "s_s", "o_out", "osq_s", "osum_s", "oroot",
                 "z_s", "y_s", "ones_s", "dch")
        s = {n: t.sem("b_" + n) for n in names}
        lev = [4 if j == 0 else LEVELS for j in tiles]
        lbase = [2 * sum(lev[:jj]) for jj in range(NJ)]
        ybase = [2 * sum(l - 1 for l in lev[:jj]) for jj in range(NJ)]
        xbase = [sum(4 * (l - 1) + 2 for l in lev[:jj]) for jj in range(NJ)]

        def x_at(jj, l, q):
            return xbase[jj] + 4 * l + ((q + 1) if l == lev[jj] - 1 else 2 * (q + 1))

        live = [jj for jj in range(NJ) if tiles[jj]]
        block = ctx.enter_context(nc.Block())

        @block.sync
        def _(sp):
            sp.dma_start(norm_spread, dram["c_norm_spread"]).then_inc(s["spread_in"], 16)
            sp.dma_start(dtb[:], rows(dram["dt_bias"], P)).then_inc(s["vec_in"], 16)
            sp.dma_start(alog[:], rows(dram["a_log"], P)).then_inc(s["vec_in"], 16)
            sp.dma_start(grow[:], rows(dram["gdn_norm"], P)).then_inc(s["vec_in"], 16)

        @block.gpsimd
        def _(pool):
            mix.pool(pool, sum(beats.values()))

        @block.scalar
        def _(act):
            for c in range(8):
                if c >= 2:
                    act.wait_ge(s["normsum"], c - 1)
                act.activation(sq[:, c % 2, :], sT[:, c, 0:TP], ACT.Square).then_inc(s["sqd"], 1)
            act.wait_ge(s["normsum"], 8)
            act.activation(root[:], bank[0:2 * 8, 4, 0:TP], ACT.Sqrt, bias=cst["eps"][0:2 * 8, :]).then_inc(s["rooted"], 1)
            for c in range(8):
                mix.act(act, act_beats.get(("n", c), 0))
            act.wait_ge(s["vec_in"], 48)
            act.activation(beta[:], rest[:, 0:NJ, B0:B0 + H], ACT.Sigmoid).then_inc(s["beta_s"], 1)
            act.activation(alog[:], alog[:], ACT.Exp).then_inc(s["alog_s"], 1)
            act.wait_ge(s["abs_s"], 1)
            act.activation(e1[:], ab[:], ACT.Exp, scale=-1.0).then_inc(s["exp_neg"], 1)
            act.wait_ge(s["abs_s"], 2)
            act.activation(l1[:], u1[:], ACT.Ln).then_inc(s["ln_s"], 1)
            act.wait_ge(s["alog_s"], 1)
            act.wait_ge(s["gc_s"], 2)
            act.activation(eg[:], gc[:], ACT.Exp).then_inc(s["eg_s"], 1)
            act.activation(kds[:], kds[:], ACT.Exp).then_inc(s["eg_s"], 1)
            act.activation(glE[:], glE[:], ACT.Exp).then_inc(s["eg_s"], 1)
            for jj, j in enumerate(tiles):
                n = SIZE[j]
                if jj:
                    act.wait_ge(s["sides_s"], jj)
                for m in range(2):
                    act.wait_ge(s["turned"], 2 * jj + m + 1)
                    act.activation((ktok if m == 0 else vtok)[0:n, :], bank[0:n, 4 + m, :],
                                   ACT.Copy).then_inc(s["turned_out"], 1)
                mix.act(act, act_beats.get(("f", jj), 0))
                act.wait_ge(s["dec_s"], jj + 1)
                act.activation(decT[0:n, :, 0:n], decT[0:n, :, 0:n], ACT.Exp).then_inc(s["dec_exp"], 1)
                for q in range(2):
                    act.activation(egB[:, 4 * q:4 * q + 4, 0:n], quad(q, P)[:, :, 0:n], ACT.Exp).then_inc(s["egb_s"], 1)
                mix.act(act, act_beats.get(("g", jj), 0) + act_beats.get(("a", jj), 0))
                for l in range(1, lev[jj]):
                    for q in range(2):
                        act.wait_ge(s["y_mm"], lbase[jj] + 2 * l + q + 1)
                        act.activation(Y[0:n, 4 * q:4 * q + 4, 0:n], quad(q, n)[:, :, 0:n],
                                       ACT.Copy).then_inc(s["y_out"], 1)
                    mix.act(act, act_beats.get(("l", jj, l), 0))
                act.wait_ge(s["uw_mm"], 2 * jj + 1)
                act.activation(u[0:n, :], bank[0:n, 0, :], ACT.Copy).then_inc(s["uw_s"], 1)
                act.wait_ge(s["uw_mm"], 2 * jj + 2)
                act.activation(wT[:, :, 0:n], quad(1, P)[:, :, 0:n], ACT.Copy).then_inc(s["uw_s"], 1)
                mix.act(act, act_beats.get(("w", jj), 0) + act_beats.get(("v", jj), 0))
                if j:
                    i = live.index(jj) + 1
                    act.activation(zs[:], rest[:, jj, Z0:Z0 + HD], ACT.Silu).then_inc(s["z_s"], 1)
                    act.wait_ge(s["o_out"], i)
                    act.activation(osq[:], y[:, j - 1, 0:HD], ACT.Square).then_inc(s["osq_s"], 1)
                    act.wait_ge(s["osum_s"], i)
                    act.activation(orm[:], orm[:], ACT.Sqrt, bias=cst["eps"][:],
                                   scale=1.0 / DK).then_inc(s["oroot"], 1)
                    act.wait_ge(s["y_s"], i)
                mix.act(act, act_beats.get(("o", jj), 0))

        @block.vector
        def _(dve):
            link = chain(dve, s["dch"])
            dve.memset(ones[:], 1.0).then_inc(s["ones_s"], 1)
            if part == 0:
                for x in (gc, kds, glE):
                    ins = dve.memset(x[:, 0, :], 0.0)
                link(ins)
            for c in range(2):
                mix.dve(dve, beats.get(("n", c), 0))
            dve.wait_ge(s["rooted"], 1)
            dve.reciprocal(root[:], root[:]).then_inc(s["inverted"], 1)
            for c in range(8):
                dve.wait_ge(s["norm_mm"], c + 1)
                dve.scalar_tensor_tensor(out=sT[:, c, 0:TP], in0=sT[:, c, 0:TP], scalar=DK ** -0.5 if c < 4 else 1.0,
                                         in1=bank[:, c % 4, 0:TP], op0=ALU.mult, op1=ALU.mult).then_inc(s["qk_scaled"], 1)
                if c + 2 < 8:
                    mix.dve(dve, beats.get(("n", c + 2), 0))
            dve.wait_ge(s["vec_in"], 48)
            link(dve.tensor_tensor(xs[:], rest[:, 0:NJ, A0:A0 + H], dtb[:].unsqueeze(1).to_broadcast([P, NJ, H]),
                                   ALU.add))
            dve.scalar_tensor_tensor(out=ab[:], in0=xs[:], scalar=-1.0, in1=xs[:], op0=ALU.mult,
                                     op1=ALU.max).then_inc(s["abs_s"], 1)
            dve.wait_ge(s["exp_neg"], 1)
            dve.tensor_scalar(u1[:], e1[:], 1.0, None, ALU.add).then_inc(s["abs_s"], 1)
            dve.wait_ge(s["abs_s"], 2)
            link(dve.scalar_tensor_tensor(out=e1[:], in0=u1[:], scalar=-1.0, in1=e1[:], op0=ALU.add, op1=ALU.subtract))
            dve.wait_ge(s["ln_s"], 1)
            link(dve.reciprocal(u1[:], u1[:]))
            link(dve.tensor_tensor(e1[:], e1[:], u1[:], ALU.mult))
            link(dve.tensor_tensor(l1[:], l1[:], e1[:], ALU.subtract))
            link(dve.scalar_tensor_tensor(out=l1[:], in0=xs[:], scalar=0.0, in1=l1[:], op0=ALU.max, op1=ALU.add))
            dve.wait_ge(s["alog_s"], 1)
            dve.scalar_tensor_tensor(out=g[:], in0=l1[:], scalar=-1.0,
                                     in1=alog[:].unsqueeze(1).to_broadcast([P, NJ, H]),
                                     op0=ALU.mult, op1=ALU.mult).then_inc(s["g_s"], 1)
            dve.wait_ge(s["g_s"], 1)
            dve.wait_ge(s["beta_s"], 1)
            dve.wait_ge(s["gates_mm"], 1)
            for jj, j in enumerate(tiles):
                n = SIZE[j]
                ins = dve.tensor_copy(gc[0:n, jj, :], bank[0:n, 4, 32 * jj:32 * jj + H])
                ins = dve.tensor_copy(glE[:, jj, :], bank[:, 4, 32 * jj + 16:32 * jj + 16 + H])
            ins.then_inc(s["gc_s"], 1)
            dve.wait_ge(s["gc_s"], 1)
            for jj, j in enumerate(tiles):
                n = SIZE[j]
                ins = dve.tensor_tensor(kds[0:n, jj, :], glE[0:n, jj, :], gc[0:n, jj, :], ALU.subtract)
            ins.then_inc(s["gc_s"], 1)
            dve.wait_ge(s["eg_s"], 3)

            def spread_gates(jj):
                n = SIZE[tiles[jj]]
                for o in range(2):
                    hs = slice(4 * o, 4 * o + 4)
                    dve.tensor_copy(gB[0:n, hs, :], g[0:n, jj, o::2].unsqueeze(2).to_broadcast([n, 4, P])
                                    ).then_inc(s["gb_s"], 1)
                    dve.tensor_copy(bB[0:n, hs, :], beta[0:n, jj, o::2].unsqueeze(2).to_broadcast([n, 4, P])
                                    ).then_inc(s["gb_s"], 1)

            dve.wait_ge(s["qk_scaled"], 8)
            spread_gates(0)
            for jj, j in enumerate(tiles):
                n = SIZE[j]
                mix.dve(dve, beats.get(("f", jj), 0))
                dve.wait_ge(s["bcast_mm"], jj + 1)
                for m, h in enumerate(ORDER):
                    ins = dve.scalar_tensor_tensor(out=decT[0:n, m, 0:n], in0=quad(m // 4, n)[:, m % 4, 0:n],
                                                   scalar=gc[0:n, jj, h:h + 1], in1=maskT[0:n, 0:n],
                                                   op0=ALU.subtract, op1=ALU.add)
                ins.then_inc(s["dec_s"], 1)
                link(dve.tensor_tensor(bg[0:n, :], beta[0:n, jj, :], eg[0:n, jj, :], ALU.mult))
                dve.wait_ge(s["turned_out"], 2 * jj + 2)

                def by_head(out, src, col):
                    return dve.tensor_tensor(out[0:n, :].rearrange("p (h d) -> p h d", h=H),
                                             src[0:n, :].rearrange("p (h d) -> p h d", h=H),
                                             col.unsqueeze(2).to_broadcast([n, H, DK]), ALU.mult)
                by_head(vb, vtok, beta[0:n, jj, :])
                by_head(kbg, ktok, bg[0:n, :])
                link(by_head(kd, ktok, kds[0:n, jj, :]))
                mix.dve(dve, beats.get(("g", jj), 0))
                dve.wait_ge(s["dec_exp"], jj + 1)
                dve.wait_ge(s["kk_mm"], 2 * jj + 2)
                for q in range(2):
                    hs = slice(4 * q, 4 * q + 4)
                    ins = dve.tensor_tensor(MT[0:n, hs, 0:n], quad(4 + q, n)[:, :, 0:n], decT[0:n, hs, 0:n], ALU.mult)
                link(ins)
                for q in range(2):
                    hs = slice(4 * q, 4 * q + 4)
                    dve.tensor_tensor(MT[0:n, hs, 0:n], MT[0:n, hs, 0:n], quad(2 + q, n)[:, :, 0:n],
                                      ALU.mult).then_inc(s["mt_s"], 1)
                dve.wait_ge(s["egb_s"], 2 * jj + 2)
                for o in (0, 1):
                    r = slice(64 * o, 64 * o + 64)
                    dve.tensor_copy(glp[r, :], glE[r, jj, o::2])
                    ins = dve.tensor_tensor(qgT[r, :, 0:n], sT[r, 0:4, START[j] - t0:START[j] - t0 + n],
                                            egB[r, 4 * o:4 * o + 4, 0:n], ALU.mult)
                ins.then_inc(s["sides_s"], 1)
                dve.wait_ge(s["sides_s"], jj + 1)
                for q in range(2):
                    hs = slice(4 * q, 4 * q + 4)
                    dve.wait_ge(s["qk_mm"], 2 * jj + q + 1)
                    dve.tensor_tensor(PT[0:n, hs, 0:n], quad(q, n)[:, :, 0:n], decT[0:n, hs, 0:n],
                                      ALU.mult).then_inc(s["pt_s"], 1)
                dve.wait_ge(s["mt_s"], 2 * jj + 2)
                dve.wait_ge(s["pt_s"], 2 * jj + 2)
                mix.dve(dve, beats.get(("a", jj), 0))

                def blocks(l):
                    for q in range(2):
                        hs = slice(4 * q, 4 * q + 4)
                        dve.tensor_tensor((BT0, BT1)[l % 2][0:n, hs, 0:n], MT[0:n, hs, 0:n],
                                          levels[0:n, l, 0:n].unsqueeze(1).to_broadcast([n, 4, n]),
                                          ALU.mult).then_inc(s["bt_s"], 1)

                blocks(0)
                for l in range(lev[jj]):
                    if l + 1 < lev[jj]:
                        blocks(l + 1)
                    for q in range(2):
                        hs = slice(4 * q, 4 * q + 4)
                        if l == 0:
                            idb = ident[0:n, 0:n].unsqueeze(1).to_broadcast([n, 4, n])
                            dve.wait_ge(s["bt_s"], lbase[jj] + 2)
                            dve.tensor_tensor(XTr[0:n, hs, 0:n], idb, BT0[0:n, hs, 0:n], ALU.subtract
                                              ).then_inc(s["x_s"], 1)
                            dve.wait_ge(s["y_mm"], lbase[jj] + q + 1)
                            dve.tensor_tensor(X[0:n, hs, 0:n], idb, quad(q, n)[:, :, 0:n], ALU.subtract
                                              ).then_inc(s["x_s"], 1)
                            continue
                        dve.wait_ge(s["xy_mm"], ybase[jj] + 2 * (l - 1) + q + 1)
                        if l < lev[jj] - 1:
                            dve.tensor_tensor(X[0:n, hs, 0:n], X[0:n, hs, 0:n], quad(2 + q, n)[:, :, 0:n],
                                              ALU.subtract).then_inc(s["x_s"], 1)
                        dve.tensor_tensor(XTr[0:n, hs, 0:n], XTr[0:n, hs, 0:n], quad(4 + q, n)[:, :, 0:n],
                                          ALU.subtract).then_inc(s["x_s"], 1)
                    dve.wait_ge(s["x_s"], x_at(jj, l, 1))
                    if l:
                        mix.dve(dve, beats.get(("l", jj, l), 0))
                if jj + 1 < NJ:
                    dve.wait_ge(s["y_out"], ybase[jj + 1])
                    spread_gates(jj + 1)
                mix.dve(dve, beats.get(("w", jj), 0))
                dve.wait_ge(s["uw_s"], 2 * jj + 2)
                if j == 0:
                    dve.tensor_copy(vn[0:n, :], u[0:n, :]).then_inc(s["vn_s"], 1)
                else:
                    i = live.index(jj) + 1
                    dve.wait_ge(s["ws_mm"], i)
                    for o, b in ((0, 2), (1, 3)):
                        ins = dve.tensor_tensor(parity(vn[0:n, :], o), parity(u[0:n, :], o),
                                                bank[0:n, b, 0:256].rearrange("p (c d) -> p c d", c=4), ALU.subtract)
                    ins.then_inc(s["vn_s"], 1)
                mix.dve(dve, beats.get(("v", jj), 0))
                upd = bank[:, 4, 0:4 * DK].rearrange("p (c e) -> p c e", c=4)
                if j == 0:
                    dve.wait_ge(s["s_mm"], jj + 1)
                    dve.tensor_copy(S[:], upd).then_inc(s["s_s"], 1)
                else:
                    dve.wait_ge(s["qs_mm"], i)
                    link(dve.tensor_tensor(S[:], S[:], glp[:].unsqueeze(2).to_broadcast([P, 4, DK]), ALU.mult))
                    dve.wait_ge(s["z_s"], i)
                    zh = zs[:].rearrange("p (h d) -> p h d", h=H)
                    link(dve.tensor_tensor(zh, zh, grow[:].unsqueeze(1).to_broadcast([P, H, DK]), ALU.mult))
                    dve.wait_ge(s["s_mm"], jj + 1)
                    dve.tensor_tensor(S[:], S[:], upd, ALU.add).then_inc(s["s_s"], 1)
                    yo = y[:, j - 1, 0:HD]
                    yh = yo.rearrange("p (h d) -> p h d", h=H)
                    dve.wait_ge(s["o_mm"], i)
                    for o, b in ((0, 0), (1, 5)):
                        ins = dve.tensor_copy(parity(yo, o), bank[:, b, 0:256].rearrange("p (c d) -> p c d", c=4))
                    ins.then_inc(s["o_out"], 1)
                    dve.wait_ge(s["osq_s"], i)
                    dve.tensor_reduce(orm[:], osq[:].rearrange("p (h d) -> p h d", h=H), AX,
                                      ALU.add).then_inc(s["osum_s"], 1)
                    dve.wait_ge(s["oroot"], i)
                    link(dve.reciprocal(orm[:], orm[:]))
                    link(dve.tensor_tensor(yh, yh, orm[:].unsqueeze(2).to_broadcast([P, H, DK]), ALU.mult))
                    dve.tensor_tensor(yo, yo, zs[:], ALU.mult).then_inc(s["y_s"], 1)
                    dve.wait_ge(s["y_s"], i)
                dve.wait_ge(s["s_s"], jj + 1)
                mix.dve(dve, beats.get(("o", jj), 0))

        @block.tensor
        def _(pe):
            for c in range(8):
                pe.wait_ge(s["sqd"], c + 1)
                pe.matmul(bank[0:2 * 8, 4, 0:TP], norm_sum[:, c, :], sq[:, c % 2, :], start=(c == 0), stop=(c == 7)
                          ).then_inc(s["normsum"], 1)
            pe.wait_ge(s["inverted"], 1)
            pe.wait_ge(s["spread_in"], 16)
            for c in range(8):
                if c >= 4:
                    pe.wait_ge(s["qk_scaled"], c - 3)
                pe.matmul(bank[:, c % 4, 0:TP], norm_spread[:, c, :], root[:], start=True, stop=True
                          ).then_inc(s["norm_mm"], 1)
                mix.pe(pe, pe_beats.get(("n", c), 0))
            pe.wait_ge(s["ones_s"], 1)
            pe.wait_ge(s["qk_scaled"], 8)
            pe.wait_ge(s["g_s"], 1)
            for jj, j in enumerate(tiles):
                n = SIZE[j]
                pe.matmul(bank[0:n, 4, 32 * jj:32 * jj + H], triu[0:n, 0:n], g[0:n, jj, :], start=True, stop=True)
                mm = pe.matmul(bank[:, 4, 32 * jj + 16:32 * jj + 16 + H], ones[0:n, :], g[0:n, jj, :],
                               start=True, stop=True)
            mm.then_inc(s["gates_mm"], 1)
            pe.wait_ge(s["gc_s"], 1)
            for jj, j in enumerate(tiles):
                n, cols = SIZE[j], slice(START[j] - t0, START[j] - t0 + SIZE[j])
                if jj:
                    pe.wait_ge(s["s_s"], jj)
                    if tiles[jj - 1]:
                        pe.wait_ge(s["o_out"], live.index(jj - 1) + 1)
                for m in range(2):
                    for c in range(4):
                        tr = pe.transpose(bank[0:n, 4 + m, c * P:(c + 1) * P], sT[:, 4 + 4 * m + c, cols], ident[:])
                    tr.then_inc(s["turned"], 1)
                pe.wait_ge(s["gb_s"], 4 * jj + 4)
                for h in range(H):
                    pe.matmul(quad(h // 4, P)[:, h % 4, 0:n], gB[0:n, h, :], triu[0:n, 0:n], start=True, stop=True)
                for h in range(H):
                    mm = pe.matmul(quad(2 + h // 4, P)[:, h % 4, 0:n], bB[0:n, h, :], ident[0:n, 0:n],
                                   start=True, stop=True)
                mm.then_inc(s["bcast_mm"], 1)
                mix.pe(pe, pe_beats.get(("f", jj), 0))
                pe.wait_ge(s["turned_out"], 2 * jj + 2)
                for m, h in enumerate(ORDER):
                    r = slice(64 * (h % 2), 64 * (h % 2) + 64)
                    mm = pe.matmul(quad(4 + m // 4, n)[:, m % 4, 0:n], sT[r, 4 + h // 2, cols], sT[r, 4 + h // 2, cols],
                                   start=True, stop=True)
                    if m % 4 == 3:
                        mm.then_inc(s["kk_mm"], 1)
                mix.pe(pe, pe_beats.get(("g", jj), 0))
                pe.wait_ge(s["egb_s"], 2 * jj + 2)
                pe.wait_ge(s["dec_s"], jj + 1)
                for m, h in enumerate(ORDER):
                    r = slice(64 * (h % 2), 64 * (h % 2) + 64)
                    mm = pe.matmul(quad(m // 4, n)[:, m % 4, 0:n], sT[r, 4 + h // 2, cols], sT[r, h // 2, cols],
                                   start=True, stop=True)
                    if m % 4 == 3:
                        mm.then_inc(s["qk_mm"], 1)
                pe.wait_ge(s["mt_s"], 2 * jj + 2)
                pe.wait_ge(s["pt_s"], 2 * jj + 2)
                mix.pe(pe, pe_beats.get(("a", jj), 0))
                for l in range(lev[jj]):
                    BT = (BT0, BT1)[l % 2]
                    for q in range(2):
                        pe.wait_ge(s["bt_s"], lbase[jj] + 2 * l + q + 1)
                        if l:
                            pe.wait_ge(s["x_s"], x_at(jj, l - 1, q))
                        for h in range(4 * q, 4 * q + 4):
                            mm = pe.matmul(quad(q, n)[:, h % 4, 0:n], BT[0:n, h, 0:n],
                                           X[0:n, h, 0:n] if l else ident[0:n, 0:n], start=True, stop=True)
                        mm.then_inc(s["y_mm"], 1)
                    if l == 0:
                        continue
                    for q in range(2):
                        pe.wait_ge(s["y_out"], ybase[jj] + 2 * (l - 1) + q + 1)
                        if l < lev[jj] - 1:
                            for h in range(4 * q, 4 * q + 4):
                                pe.matmul(quad(2 + q, n)[:, h % 4, 0:n], XTr[0:n, h, 0:n], Y[0:n, h, 0:n],
                                          start=True, stop=True)
                        for h in range(4 * q, 4 * q + 4):
                            mm = pe.matmul(quad(4 + q, n)[:, h % 4, 0:n], Y[0:n, h, 0:n], XTr[0:n, h, 0:n],
                                           start=True, stop=True)
                        mm.then_inc(s["xy_mm"], 1)
                    mix.pe(pe, pe_beats.get(("l", jj, l), 0))
                pe.wait_ge(s["x_s"], x_at(jj, lev[jj] - 1, 1))
                pe.wait_ge(s["sides_s"], jj + 1)
                for m, h in enumerate(ORDER):
                    mm = pe.matmul(bank[0:n, 0, h * DK:(h + 1) * DK], XTr[0:n, m, 0:n], vb[0:n, h * DK:(h + 1) * DK],
                                   start=True, stop=True)
                mm.then_inc(s["uw_mm"], 1)
                for m, h in enumerate(ORDER):
                    r = slice(64 * (h % 2), 64 * (h % 2) + 64)
                    mm = pe.matmul(quad(1, P)[r, h // 2, 0:n], kbg[0:n, h * DK:(h + 1) * DK], XTr[0:n, m, 0:n],
                                   start=True, stop=True)
                mm.then_inc(s["uw_mm"], 1)
                mix.pe(pe, pe_beats.get(("w", jj), 0))
                if j:
                    pe.wait_ge(s["uw_s"], 2 * jj + 2)
                    for h in range(H):
                        r = slice(64 * (h % 2), 64 * (h % 2) + 64)
                        mm = pe.matmul(bank[0:n, (2, 3)[h % 2], (h // 2) * DK:(h // 2 + 1) * DK], wT[r, h // 2, 0:n],
                                       S[r, h // 2, :], start=True, stop=True)
                    mm.then_inc(s["ws_mm"], 1)
                if j:
                    for h in range(H):
                        r = slice(64 * (h % 2), 64 * (h % 2) + 64)
                        mm = pe.matmul(bank[0:n, (0, 5)[h % 2], (h // 2) * DK:(h // 2 + 1) * DK], qgT[r, h // 2, 0:n],
                                       S[r, h // 2, :], start=(h < 2), stop=False, skip_group_check=True)
                    mm.then_inc(s["qs_mm"], 1)
                mix.pe(pe, pe_beats.get(("v", jj), 0))
                pe.wait_ge(s["vn_s"], jj + 1)
                for h in range(H):
                    r = slice(64 * (h % 2), 64 * (h % 2) + 64)
                    mm = pe.matmul(bank[r, 4, (h // 2) * DK:(h // 2) * DK + DK], kd[0:n, h * DK:(h + 1) * DK],
                                   vn[0:n, h * DK:(h + 1) * DK], start=True, stop=True)
                mm.then_inc(s["s_mm"], 1)
                if j:
                    for m, h in enumerate(ORDER):
                        mm = pe.matmul(bank[0:n, (0, 5)[h % 2], (h // 2) * DK:(h // 2 + 1) * DK], PT[0:n, m, 0:n],
                                       vn[0:n, h * DK:(h + 1) * DK], start=False, stop=True, skip_group_check=True)
                    mm.then_inc(s["o_mm"], 1)
                mix.pe(pe, pe_beats.get(("o", jj), 0))


def latent_attention(nc, dram, cst, keep, mix, part, beats):
    with ExitStack() as ctx:
        t = Tools(nc, ctx)
        act_beats, pe_beats = mix.later(beats, 1), mix.later(beats, 2)
        rest, y, ident, mask = keep["rest"], keep["y"], cst["ident"], cst["mask"]
        LAT, VD = QL + KL, 64
        tiles = PARTS[part]
        NJ = len(tiles)
        kT, V = keep["kT"], keep["V"]
        wuq, wukv = t.sb("w_uq_s", [P, 2, H * QKD]), t.sb("w_ukv_s", [P, H * P])
        lrow, nrow = t.sb("latent_rows", [P, LAT]), t.sb("head_rows", [P, 2, QKD])
        ls, junk = t.sb("ls", [P, 2 * NJ]), t.sb("lat_junk", [P, LAT])
        cn = t.sb("cn", [P, LAT])
        cT = t.sb("cT", [P, 3, P])
        QKs, QKsq = t.sb("QK", [P, 2, 2, H, QKD]), t.sb("QKsq", [P, 2, H, QKD])
        qks = t.sb("qks", [P, 2, H])
        ra, rb = t.sb("ra", [P, 2, H, 16]), t.sb("rb", [P, 2, H, 16])
        rc, rd = t.sb("rc", [P, 2, H, 16]), t.sb("rd", [P, 2, H, 16])
        qT = t.sb("qT", [QKD, H, 2 * P])
        nm, mx, rsum = t.sb("nm", [P, 2]), t.sb("mx", [P, 2]), t.sb("rsum", [P, 2, H])
        rinv = t.sb("rinv", [P, H])
        pm, pT = t.sb("probs", [P, 2, T]), t.sb("probsT", [P, 2, NT, P])
        bank = t.ps("mla_banks", [P, 6, 512])
        names = ("rows_in", "nrows_in", "w_in", "lsq", "lroot", "cn_s", "ct_mm", "ct_s", "qkv_mm", "v_s", "qk_sq", "qk_sum",
                 "qk_root", "rope_s", "tr_mm", "tr_s", "s_mm", "max_s", "exp_s", "pt_mm", "pt_s",
                 "o_mm", "o_s", "dch")
        s = {n: t.sem("c_" + n) for n in names}
        units = [(j, h) for j in tiles if j for h in range(H)]
        xt = [j for j in tiles if j]
        KCOL = lambda j: SEQ if j == 0 else (j - 1) * P
        turns = [(jj, side, q) for jj, j in enumerate(tiles) for side in ((1,) if j == 0 else (0, 1)) for q in range(2)]
        upto = [sum(1 for x in turns if x[0] <= jj) for jj in range(NJ)]
        ropes = [sum(1 if j == 0 else 2 for j in tiles[:jj + 1]) for jj in range(NJ)]
        block = ctx.enter_context(nc.Block())

        @block.sync
        def _(sp):
            sp.dma_start(lrow[:, 0:QL], rows(dram["q_a_norm"], P)).then_inc(s["rows_in"], 16)
            sp.dma_start(lrow[:, QL:LAT], rows(dram["kv_a_norm"], P)).then_inc(s["rows_in"], 16)
            sp.dma_start(wuq[:], dram["w_uq"].rearrange("(k p) n -> p k n", p=P)).then_inc(s["w_in"], 16)
            sp.dma_start(wukv[:], dram["w_ukv"]).then_inc(s["w_in"], 16)
            sp.dma_start(nrow[:, 0, :], rows(dram["q_norm"], P)).then_inc(s["nrows_in"], 16)
            sp.dma_start(nrow[:, 1, :], rows(dram["k_norm"], P)).then_inc(s["nrows_in"], 16)

        @block.gpsimd
        def _(pool):
            mix.pool(pool, sum(beats.values()))

        @block.scalar
        def _(act):
            link = chain(act, s["lsq"])
            for jj, j in enumerate(tiles):
                n = SIZE[j]
                link(act.activation(junk[0:n, 0:QL], rest[0:n, jj, CQ0:CQ0 + QL], ACT.Square,
                                    accum_out=ls[0:n, 2 * jj:2 * jj + 1]))
                link(act.activation(junk[0:n, QL:LAT], rest[0:n, jj, CKV0:CKV0 + KL], ACT.Square,
                                    accum_out=ls[0:n, 2 * jj + 1:2 * jj + 2]))
                act.activation(ls[0:n, 2 * jj:2 * jj + 1], ls[0:n, 2 * jj:2 * jj + 1], ACT.Sqrt, bias=cst["eps"][0:n, :],
                               scale=1.0 / QL).then_inc(s["lroot"], 1)
                act.activation(ls[0:n, 2 * jj + 1:2 * jj + 2], ls[0:n, 2 * jj + 1:2 * jj + 2], ACT.Sqrt,
                               bias=cst["eps"][0:n, :], scale=1.0 / KL).then_inc(s["lroot"], 1)
            for jj, j in enumerate(tiles):
                n, lo, QK = SIZE[j], (1 if j == 0 else 0), QKs[:, jj % 2, :, :, :]
                act.wait_ge(s["qkv_mm"], jj + 1)
                if jj >= 2:
                    act.wait_ge(s["tr_mm"], upto[jj - 2])
                if j:
                    link(act.activation(QK[0:n, 0, :, :].rearrange("p h d -> p (h d)").rearrange("p (a c) -> p a c", a=2),
                                        bank[0:n, 0:2, 0:384], ACT.Copy))
                kv = bank[0:n, 2:4, :].rearrange("p a (h d) -> p (a h) d", d=P)
                link(act.activation(QK[0:n, 1, :, 0:NOPE], kv[:, :, 0:NOPE], ACT.Copy))
                act.activation(V[0:n, j, :, :], kv[:, :, NOPE:P], ACT.Copy).then_inc(s["v_s"], 1)
                link(act.activation(QK[0:n, 1, :, NOPE:QKD],
                                    rest[0:n, jj, KPE0:KPE0 + ROPE].unsqueeze(1).to_broadcast([n, H, ROPE]), ACT.Copy))
                act.activation(QKsq[0:n, lo:, :, :], QK[0:n, lo:, :, :], ACT.Square).then_inc(s["qk_sq"], 1)
                act.wait_ge(s["qk_sum"], jj + 1)
                act.activation(qks[0:n, lo:, :], qks[0:n, lo:, :], ACT.Sqrt, bias=cst["eps"][0:n, :],
                               scale=1.0 / QKD).then_inc(s["qk_root"], 1)
                mix.act(act, sum(act_beats.get((k, jj), 0) for k in "prt"))
            for i in range(len(units) + 1):
                if i:
                    tt, h = units[i - 1]
                    act.wait_ge(s["pt_mm"], i)
                    if i >= 3:
                        act.wait_ge(s["o_mm"], i - 2)
                    act.activation(pT[:, (i - 1) % 2, 0:tt, :], bank[:, 4, 0:P * tt].rearrange("p (a b) -> p a b", b=P),
                                   ACT.Copy).then_inc(s["pt_s"], 1)
                    act.activation(pT[0:META, (i - 1) % 2, NT - 1, :], bank[0:META, 2 * ((i - 1) % 2) + 1, 256:256 + P],
                                   ACT.Copy).then_inc(s["pt_s"], 1)
                if i < len(units):
                    tt, h = units[i]
                    act.wait_ge(s["max_s"], i + 1)
                    if i >= 2:
                        act.wait_ge(s["pt_mm"], i - 1)
                    act.activation(pm[:, i % 2, 0:P * tt + META], bank[:, 2 * (i % 2):2 * (i % 2) + 2, :].rearrange(
                        "p a b -> p (a b)")[:, 0:P * tt + META], ACT.Exp, bias=nm[:, i % 2:i % 2 + 1], scale=SCALE,
                        accum_out=rsum[:, tt % 2, h:h + 1]).then_inc(s["exp_s"], 1)
                if i:
                    mix.act(act, act_beats.get(("u", i - 1), 0))

        @block.vector
        def _(dve):
            link = chain(dve, s["dch"])
            dve.wait_ge(s["rows_in"], 32)

            def latent(jj):
                n = SIZE[tiles[jj]]
                dve.wait_ge(s["lroot"], 2 * jj + 2)
                link(dve.reciprocal(ls[0:n, 2 * jj:2 * jj + 2], ls[0:n, 2 * jj:2 * jj + 2]))
                if jj:
                    dve.wait_ge(s["ct_mm"], jj)
                dve.scalar_tensor_tensor(out=cn[0:n, 0:QL], in0=rest[0:n, jj, CQ0:CQ0 + QL],
                                         scalar=ls[0:n, 2 * jj:2 * jj + 1], in1=lrow[0:n, 0:QL],
                                         op0=ALU.mult, op1=ALU.mult).then_inc(s["cn_s"], 1)
                dve.scalar_tensor_tensor(out=cn[0:n, QL:LAT], in0=rest[0:n, jj, CKV0:CKV0 + KL],
                                         scalar=ls[0:n, 2 * jj + 1:2 * jj + 2], in1=lrow[0:n, QL:LAT],
                                         op0=ALU.mult, op1=ALU.mult).then_inc(s["cn_s"], 1)

            def latent_out(jj):
                n = SIZE[tiles[jj]]
                dve.wait_ge(s["ct_mm"], jj + 1)
                if jj:
                    dve.wait_ge(s["qkv_mm"], jj)
                dve.tensor_copy(cT[:, :, 0:n], bank[:, 4, 0:3 * P].rearrange("p (a b) -> p a b", a=3)[:, :, 0:n]
                                ).then_inc(s["ct_s"], 1)

            latent(0)
            latent_out(0)
            dve.wait_ge(s["nrows_in"], 32)
            done = 0
            for jj, j in enumerate(tiles):
                n, lo, QK = SIZE[j], (1 if j == 0 else 0), QKs[:, jj % 2, :, :, :]
                if jj + 1 < NJ:
                    latent(jj + 1)
                    latent_out(jj + 1)
                hs = slice(lo, 2)
                mix.dve(dve, beats.get(("p", jj), 0))
                dve.wait_ge(s["qk_sq"], jj + 1)
                dve.tensor_reduce(qks[0:n, hs, :], QKsq[0:n, hs, :, :], AX, ALU.add).then_inc(s["qk_sum"], 1)
                dve.wait_ge(s["qk_root"], jj + 1)
                link(dve.reciprocal(qks[0:n, hs, :], qks[0:n, hs, :]))
                for side in range(lo, 2):
                    link(dve.tensor_tensor(QK[0:n, side, :, :], QK[0:n, side, :, :],
                                           qks[0:n, side, :].unsqueeze(2).to_broadcast([n, H, QKD]), ALU.mult))
                    link(dve.tensor_tensor(QK[0:n, side, :, :], QK[0:n, side, :, :],
                                           nrow[0:n, side, :].unsqueeze(1).to_broadcast([n, H, QKD]), ALU.mult))
                    cos = cst["cos"][0:n, j, :].unsqueeze(1).to_broadcast([n, H, 16])
                    sin = cst["sin"][0:n, j, :].unsqueeze(1).to_broadcast([n, H, 16])
                    x1, x2 = QK[0:n, side, :, NOPE:NOPE + 16], QK[0:n, side, :, NOPE + 16:QKD]
                    dve.tensor_tensor(ra[0:n, side, :, :], x1, cos, ALU.mult)
                    dve.tensor_tensor(rb[0:n, side, :, :], x2, sin, ALU.mult)
                    dve.tensor_tensor(rc[0:n, side, :, :], x2, cos, ALU.mult)
                    link(dve.tensor_tensor(rd[0:n, side, :, :], x1, sin, ALU.mult))
                    dve.tensor_tensor(x1, ra[0:n, side, :, :], rb[0:n, side, :, :], ALU.subtract)
                    dve.tensor_tensor(x2, rc[0:n, side, :, :], rd[0:n, side, :, :], ALU.add).then_inc(s["rope_s"], 1)
                    if side == 0:
                        mix.dve(dve, beats.get(("r", jj), 0))
                for side in range(lo, 2):
                    for q in range(2):
                        dve.wait_ge(s["tr_mm"], done + 1)
                        dst = (kT if side else qT)[:, 4 * q:4 * q + 4, :]
                        c0 = KCOL(j) if side else P * (jj - NJ + 2)
                        dve.tensor_copy(dst[:, :, c0:c0 + n],
                                        bank[0:QKD, 4 + done % 2, :].rearrange("p (a b) -> p a b", a=4)[:, :, 0:n]
                                        ).then_inc(s["tr_s"], 1)
                        done += 1
                mix.dve(dve, beats.get(("t", jj), 0))
            for i, (tt, h) in enumerate(units):
                sc = bank[:, 2 * (i % 2):2 * (i % 2) + 2, :].rearrange("p a b -> p (a b)")
                dve.wait_ge(s["s_mm"], i + 1)
                if i >= 2:
                    dve.wait_ge(s["exp_s"], i - 1)
                diag = sc[:, P * (tt - 1):P * tt]
                link(dve.tensor_tensor(diag, diag, mask[:], ALU.add))
                link(dve.tensor_reduce(mx[:, i % 2:i % 2 + 1], sc[:, 0:P * tt + META], AX, ALU.max))
                dve.tensor_scalar(nm[:, i % 2:i % 2 + 1], mx[:, i % 2:i % 2 + 1], -SCALE, None,
                                  ALU.mult).then_inc(s["max_s"], 1)
                if i:
                    mix.dve(dve, beats.get(("u", i - 1), 0))
                if (h == 0 and i) or i == len(units) - 1:
                    td = units[i - 1][0] if h == 0 else tt
                    done_units = H * (xt.index(td) + 1)
                    dve.wait_ge(s["o_mm"], done_units)
                    dve.wait_ge(s["exp_s"], done_units)
                    link(dve.reciprocal(rinv[:], rsum[:, td % 2, :]))
                    dve.tensor_tensor(y[:, td - 1, 512:D].rearrange("p (h d) -> p h d", h=H),
                                      bank[:, 5, :].rearrange("p (h d) -> p h d", h=H),
                                      rinv[:].unsqueeze(2).to_broadcast([P, H, VD]), ALU.mult).then_inc(s["o_s"], 1)
                    dve.wait_ge(s["o_s"], xt.index(td) + 1)
            mix.dve(dve, beats.get(("u", len(units) - 1), 0))

        @block.tensor
        def _(pe):
            done = 0

            def expand(jj):
                n, j = SIZE[tiles[jj]], tiles[jj]
                pe.wait_ge(s["cn_s"], 2 * jj + 2)
                if jj >= 2:
                    pe.wait_ge(s["tr_s"], upto[jj - 2])
                for c in range(3):
                    tr = pe.transpose(bank[:, 4, c * P:c * P + n], cn[0:n, c * P:(c + 1) * P], ident[0:n, 0:n])
                tr.then_inc(s["ct_mm"], 1)
                pe.wait_ge(s["ct_s"], jj + 1)
                if jj == 0:
                    pe.wait_ge(s["w_in"], 32)
                if jj:
                    pe.wait_ge(s["qk_sq"], jj)
                    pe.wait_ge(s["v_s"], jj)
                if j:
                    for a in range(2):
                        for c in range(2):
                            pe.matmul(bank[0:n, a, 0:384], cT[:, c, 0:n], wuq[:, c, 384 * a:384 * a + 384],
                                      start=(c == 0), stop=(c == 1))
                for a in range(2):
                    mm = pe.matmul(bank[0:n, 2 + a, :], cT[:, 2, 0:n], wukv[:, 512 * a:512 * a + 512],
                                   start=True, stop=True)
                mm.then_inc(s["qkv_mm"], 1)

            expand(0)
            for jj, j in enumerate(tiles):
                if jj + 1 < NJ:
                    expand(jj + 1)
                mix.pe(pe, pe_beats.get(("p", jj), 0) + pe_beats.get(("r", jj), 0))
                n, QK = SIZE[j], QKs[:, jj % 2, :, :, :]
                lo = 1 if j == 0 else 0
                pe.wait_ge(s["rope_s"], ropes[jj])
                for side in range(lo, 2):
                    for q in range(2):
                        if done >= 2:
                            pe.wait_ge(s["tr_s"], done - 1)
                        for h in range(4):
                            tr = pe.transpose(bank[0:QKD, 4 + done % 2, h * P:h * P + n], QK[0:n, side, 4 * q + h, :],
                                              ident[0:n, 0:n])
                        tr.then_inc(s["tr_mm"], 1)
                        done += 1
                mix.pe(pe, pe_beats.get(("t", jj), 0))
            pe.wait_ge(s["tr_s"], len(turns))
            pe.wait_ge(s["v_s"], NJ)

            def score(i):
                tt, h = units[i]
                if i >= 2:
                    pe.wait_ge(s["exp_s"], i - 1)
                q = qT[:, h, P * xt.index(tt):P * (xt.index(tt) + 1)]
                b0, off = (2 * (i % 2), P * tt) if tt < XT else (2 * (i % 2) + 1, 0)
                pe.matmul(bank[:, 2 * (i % 2), 0:P * tt], q, kT[:, h, 0:P * tt], start=True, stop=True)
                pe.matmul(bank[:, b0, off:off + META], q, kT[:, h, SEQ:T], start=True, stop=True).then_inc(s["s_mm"], 1)

            score(0)
            for i, (tt, h) in enumerate(units):
                if i + 1 < len(units):
                    score(i + 1)
                pe.wait_ge(s["exp_s"], i + 1)
                if i:
                    pe.wait_ge(s["pt_s"], 2 * i)
                for c in range(tt):
                    pe.transpose(bank[:, 4, c * P:(c + 1) * P], pm[:, i % 2, c * P:(c + 1) * P], ident[:])
                pe.transpose(bank[0:META, 2 * (i % 2) + 1, 256:256 + P], pm[:, i % 2, P * tt:P * tt + META], ident[:]).then_inc(s["pt_mm"], 1)
                n = pe_beats.get(("u", i), 0)
                mix.pe(pe, n // 2)
                pe.wait_ge(s["pt_s"], 2 * i + 2)
                if h == 0 and i:
                    pe.wait_ge(s["o_s"], xt.index(tt))
                o = bank[:, 5, h * VD:(h + 1) * VD]
                for c in range(tt):
                    pe.matmul(o, pT[:, i % 2, c, :], V[:, c + 1, h, :], start=(c == 0), stop=False)
                pe.matmul(o, pT[0:META, i % 2, NT - 1, :], V[0:META, 0, h, :], start=False, stop=True
                          ).then_inc(s["o_mm"], 1)
                mix.pe(pe, n - n // 2)


def out_project(nc, dram, cst, y, h1, W, mix, part, beats):
    with ExitStack() as ctx:
        t = Tools(nc, ctx)
        act_beats, pe_beats = mix.later(beats, 1), mix.later(beats, 2)
        ident = cst["ident"]
        xt = [j - 1 for j in PARTS[part] if j]
        N, NB = len(xt), D // WCOLS
        yT, frow, fs = t.sb("yT", [P, N, KD, P]), t.sb("ffn_row", [P, D]), t.sb("fs", [P, N])
        tb, hb = t.ps("yT_banks", [P, 2, 512]), t.ps("h1_banks", [P, 4, 512])
        jobs = [(a, i) for a in range(NB) for i in range(N)]
        names = ("x_full", "yt_mm", "yt_s", "h_mm", "h_s", "sq_s", "root", "xn_s", "dch")
        s = {n: t.sem("d_" + n) for n in names}
        block = ctx.enter_context(nc.Block())

        @block.sync
        def _(sp):
            sp.dma_start(h1[:, xt[0]:xt[0] + N, :],
                         dram["x"][xt[0] * P:(xt[0] + N) * P, :].rearrange("(t p) d -> p t d", p=P)
                         ).then_inc(s["x_full"], 16)
            sp.dma_start(frow[:], rows(dram["ffn_norm"], P)).then_inc(s["x_full"], 16)
            W.load(sp, [(s["h_mm"], N * (a + 1)) for a in range(NB)])

        @block.gpsimd
        def _(pool):
            mix.pool(pool, sum(beats.values()))

        @block.tensor
        def _(pe):
            for m in range(2 * N):
                i, half = m // 2, m % 2
                if m >= 2:
                    pe.wait_ge(s["yt_s"], m - 1)
                for k in range(4):
                    tr = pe.transpose(tb[:, half, k * P:(k + 1) * P],
                                      y[:, xt[i], (4 * half + k) * P:(4 * half + k + 1) * P], ident[:])
                tr.then_inc(s["yt_mm"], 1)
            pe.wait_ge(s["yt_s"], 2 * N)
            for m, (a, i) in enumerate(jobs):
                if i == 0:
                    w = W.take(pe)
                if m >= 4:
                    pe.wait_ge(s["h_s"], m - 3)
                for k in range(KD):
                    mm = pe.matmul(hb[:, m % 4, 0:WCOLS], yT[:, i, k, :], w[:, k, :], start=(k == 0), stop=(k == KD - 1))
                mm.then_inc(s["h_mm"], 1)
                mix.pe(pe, pe_beats.get(m, 0))

        @block.scalar
        def _(act):
            for m in range(2 * N):
                i, half = m // 2, m % 2
                act.wait_ge(s["yt_mm"], m + 1)
                act.activation(yT[:, i, 4 * half:4 * half + 4, :], tb[:, half, :].rearrange("p (a b) -> p a b", a=4),
                               ACT.Copy).then_inc(s["yt_s"], 1)
            for m in range(len(jobs)):
                mix.act(act, act_beats.get(m, 0))
            for i in range(N):
                act.wait_ge(s["h_s"], len(jobs) - N + i + 1)
                act.activation(y[:, xt[i], :], h1[:, xt[i], :], ACT.Square, accum_out=fs[:, i:i + 1]
                               ).then_inc(s["sq_s"], 1)
                act.wait_ge(s["sq_s"], i + 1)
                act.activation(fs[:, i:i + 1], fs[:, i:i + 1], ACT.Sqrt, bias=cst["eps"][:],
                               scale=1.0 / D).then_inc(s["root"], 1)

        @block.vector
        def _(dve):
            link = chain(dve, s["dch"])
            dve.wait_ge(s["x_full"], 32)
            for m, (a, i) in enumerate(jobs):
                dve.wait_ge(s["h_mm"], m + 1)
                part_row = h1[:, xt[i], a * WCOLS:(a + 1) * WCOLS]
                dve.tensor_tensor(part_row, part_row, hb[:, m % 4, 0:WCOLS], ALU.add).then_inc(s["h_s"], 1)
                mix.dve(dve, beats.get(m, 0))
            for i in range(N):
                dve.wait_ge(s["root"], i + 1)
                link(dve.reciprocal(fs[:, i:i + 1], fs[:, i:i + 1]))
                dve.scalar_tensor_tensor(out=y[:, xt[i], :], in0=h1[:, xt[i], :], scalar=fs[:, i:i + 1], in1=frow[:],
                                         op0=ALU.mult, op1=ALU.mult).then_inc(s["xn_s"], 1)


class Choice:
    def __init__(self, t, cst, scores, idx, gates, tt):
        K, B = TOPK, 4
        self.K, self.B, self.LOW = K, B, -3.0e38
        self.cst, self.scores, self.idx, self.gates, self.tt = cst, scores, idx, gates, tt
        self.left = t.sb("left", [P, B, KEYS])
        self.sv, self.si = t.sb("sv", [P, 2 * B, K]), t.sb("si", [P, 2 * B, K], U32)
        self.sif = t.sb("sif", [P, 2 * B, K])
        self.cand, self.cleft = t.sb("cand", [P, B, K, K]), t.sb("cleft", [P, B, K * K])
        self.cv, self.ci = t.sb("cv", [P, B, K]), t.sb("ci", [P, B, K], U32)
        self.ab, self.abf = t.sb("ab_i", [P, 2, B, K], U32), t.sb("ab_f", [P, 2, B, K])
        self.hot = t.sb("hot", [P, B * K, K])
        self.pick = t.sb("pick", [P, 2, B * K])
        self.gsum = t.sb("gsum", [P, B])
        self.dch, self.cv_s, self.exp_s, self.ready = (t.sem("f_" + n) for n in ("dch", "cv", "exp", "ready"))

    def here(self, g):
        n = self.B * self.K
        return slice(self.tt * SLOTS + g * n, self.tt * SLOTS + (g + 1) * n)

    def start(self, dve):
        self.link = chain(dve, self.dch)

    def top16(self, dve, srcs, lefts, vals, inds):
        n, link = len(srcs), self.link
        for i in range(n):
            ins = dve.max(vals[i][:, 0:8], srcs[i])
        link(ins)
        for i in range(n):
            dve.max_index(inds[i][:, 0:8], vals[i][:, 0:8], srcs[i])
            ins = dve.match_replace(lefts[i], vals[i][:, 0:8], srcs[i], self.LOW)
        link(ins)
        for i in range(n):
            ins = dve.max(vals[i][:, 8:16], lefts[i])
        link(ins)
        for i in range(n):
            ins = dve.max_index(inds[i][:, 8:16], vals[i][:, 8:16], lefts[i])
        link(ins)

    def halves(self, dve, g, part):
        B, b = self.B, part * self.B
        self.top16(dve, [self.scores[:, self.tt % 2, 2 * B * g + b + i, :] for i in range(B)],
                   [self.left[:, i, :] for i in range(B)],
                   [self.sv[:, b + i, :] for i in range(B)], [self.si[:, b + i, :] for i in range(B)])

    def pairs(self, dve, g):
        B, K, sv = self.B, self.K, self.sv
        dve.tensor_copy(self.sif[:], self.si[:])
        for i in range(B):
            ins = dve.tensor_tensor(self.cand[:, i, :, :], sv[:, 2 * i, :].unsqueeze(2).to_broadcast([P, K, K]),
                                    sv[:, 2 * i + 1, :].unsqueeze(1).to_broadcast([P, K, K]), ALU.add)
        self.link(ins)
        self.top16(dve, [self.cand[:, i, :, :].rearrange("p a b -> p (a b)") for i in range(B)],
                   [self.cleft[:, i, :] for i in range(B)],
                   [self.cv[:, i, :] for i in range(B)], [self.ci[:, i, :] for i in range(B)])
        gt = self.gates[:, self.here(g)].rearrange("p (h k) -> p h k", h=B)
        dve.tensor_tensor(gt, self.cv[:], self.cv[:, :, 0:1].to_broadcast([P, B, K]), ALU.subtract).then_inc(self.cv_s, 1)
        dve.tensor_scalar(self.ab[:, 0, :, :], self.ci[:], 4, None, ALU.logical_shift_right)
        self.link(dve.tensor_scalar(self.ab[:, 1, :, :], self.ci[:], 15, None, ALU.bitwise_and))
        self.link(dve.tensor_copy(self.abf[:], self.ab[:]))

    def sub_keys(self, dve, o):
        B, K, link, hot = self.B, self.K, self.link, self.hot
        link(dve.tensor_tensor(hot[:], self.abf[:, o, :, :].rearrange("p h k -> p (h k)").unsqueeze(2)
                               .to_broadcast([P, B * K, K]),
                               self.cst["iota16"][:].unsqueeze(1).to_broadcast([P, B * K, K]), ALU.is_equal))
        hv = hot[:].rearrange("p (h k) a -> p h k a", h=B)
        link(dve.tensor_tensor(hv, hv, self.sif[:, o::2, :].unsqueeze(2).to_broadcast([P, B, K, K]), ALU.mult))
        link(dve.tensor_reduce(self.pick[:, o, :], hot[:], AX, ALU.add))

    def exps(self, act, g):
        gt = self.gates[:, self.here(g)]
        act.wait_ge(self.cv_s, g + 1)
        act.activation(gt, gt, ACT.Exp).then_inc(self.exp_s, 1)

    def rows(self, dve, g):
        B, K, link = self.B, self.K, self.link
        gt = self.gates[:, self.here(g)].rearrange("p (h k) -> p h k", h=B)
        link(dve.scalar_tensor_tensor(out=self.idx[:, self.here(g)], in0=self.pick[:, 0, :], scalar=float(KEYS),
                                      in1=self.pick[:, 1, :], op0=ALU.mult, op1=ALU.add))
        dve.wait_ge(self.exp_s, g + 1)
        link(dve.tensor_reduce(self.gsum[:], gt, AX, ALU.add))
        link(dve.reciprocal(self.gsum[:], self.gsum[:]))
        dve.tensor_tensor(gt, gt, self.gsum[:].unsqueeze(2).to_broadcast([P, B, K]), ALU.mult).then_inc(self.ready, 1)
        dve.wait_ge(self.ready, g + 1)


def score_and_choose(nc, dram, cst, xn, scores, idx, gates, W, mix, part, beats, own):
    with ExitStack() as ctx:
        t = Tools(nc, ctx)
        act_beats, pe_beats = mix.later(beats, 1), mix.later(beats, 2)
        ident, HP = cst["ident"], 2 * H
        xt = [j - 1 for j in PARTS[part] if j]
        N = len(xt)
        keys, keysT = t.sb("keys", [P, HP, P]), t.sb("keysT", [P, HP, P])
        xnT, qT = t.sb("xnT", [P, KD, N * P]), t.sb("peer_qT", [P, 2, N * P])
        bank = t.ps("key_banks", [P, 6, 512])
        names = ("k_full", "tr_mm", "tr_s", "q_mm", "q_s", "sc_mm", "sc_s")
        s = {n: t.sem("e_" + n) for n in names}
        choice = Choice(t, cst, scores, idx, gates, xt[0])
        turns = [(xnT[:, 4 * g:4 * g + 4, P * i:P * (i + 1)], [xn[:, xt[i], P * (4 * g + k):P * (4 * g + k + 1)] for k in range(4)])
                 for i in range(N) for g in range(2)]
        turns += [(keysT[:, 4 * g:4 * g + 4, :], [keys[:, 4 * g + k, :] for k in range(4)]) for g in range(HP // 4)]
        block = ctx.enter_context(nc.Block())

        @block.sync
        def _(sp):
            sp.dma_start(keys[:], dram["sub_keys"].rearrange("h s k c -> k (h s) c")).then_inc(s["k_full"], 16)
            W.load(sp, [(s["q_mm"], 2 * (a + 1)) for a in range(H)])

        @block.gpsimd
        def _(pool):
            if own:
                pool.wait_ge(choice.ready, 1)
            mix.pool(pool, sum(beats.values()))

        @block.tensor
        def _(pe):
            for m, (_, blocks) in enumerate(turns):
                if m == 2 * N:
                    pe.wait_ge(s["k_full"], 16)
                if m >= 2:
                    pe.wait_ge(s["tr_s"], m - 1)
                for k, b in enumerate(blocks):
                    tr = pe.transpose(bank[:, m % 2, k * P:(k + 1) * P], b, ident[:])
                tr.then_inc(s["tr_mm"], 1)
            pe.wait_ge(s["tr_s"], len(turns))
            for i in range(HP + 1):
                if i < HP:
                    if i % 2 == 0:
                        w = W.take(pe)
                    if i >= 2:
                        pe.wait_ge(s["q_s"], i - 1)
                    for k in range(KD):
                        mm = pe.matmul(bank[:, 2 + i % 2, 0:N * P], w[:, k, (i % 2) * P:(i % 2 + 1) * P], xnT[:, k, :],
                                       start=(k == 0), stop=(k == KD - 1))
                    mm.then_inc(s["q_mm"], 1)
                if i:
                    j = i - 1
                    pe.wait_ge(s["q_s"], j + 1)
                    if j >= 2:
                        pe.wait_ge(s["sc_s"], j - 1)
                    for tt in range(N):
                        mm = pe.matmul(bank[:, 4 + j % 2, tt * P:(tt + 1) * P], qT[:, j % 2, tt * P:(tt + 1) * P],
                                       keysT[:, j, :], start=True, stop=True)
                    mm.then_inc(s["sc_mm"], 1)
                    mix.pe(pe, pe_beats.get(j, 0))
            mix.pe(pe, sum(pe_beats.get(k, 0) for k in range(HP, HP + 4)))

        @block.scalar
        def _(act):
            for i in range(HP + 1):
                if i < HP:
                    act.wait_ge(s["q_mm"], i + 1)
                    if i >= 2:
                        act.wait_ge(s["sc_mm"], i - 1)
                    act.activation(qT[:, i % 2, :], bank[:, 2 + i % 2, 0:N * P], ACT.Copy).then_inc(s["q_s"], 1)
                if i:
                    j = i - 1
                    act.wait_ge(s["sc_mm"], j + 1)
                    act.activation(scores[:, :, j, :], bank[:, 4 + j % 2, 0:N * P].rearrange("p (a b) -> p a b", a=N),
                                   ACT.Copy).then_inc(s["sc_s"], 1)
                    if own and j == 12:
                        act.wait_ge(choice.ready, 1)
                    mix.act(act, act_beats.get(j, 0))
                    if j == 10:
                        choice.exps(act, 0)
            mix.act(act, act_beats.get(HP, 0) + act_beats.get(HP + 1, 0))
            choice.exps(act, 1)
            mix.act(act, act_beats.get(HP + 2, 0) + act_beats.get(HP + 3, 0))

        @block.vector
        def _(dve):
            for m, (dst, _) in enumerate(turns):
                dve.wait_ge(s["tr_mm"], m + 1)
                dve.tensor_copy(dst, bank[:, m % 2, :].rearrange("p (a b) -> p a b", a=4)).then_inc(s["tr_s"], 1)
            choice.start(dve)
            for j in range(HP):
                mix.dve(dve, beats.get(j, 0))
                if j == 11:
                    choice.rows(dve, 0)
                if j % 4 == 3:
                    dve.wait_ge(s["sc_s"], j + 1)
                    choice.halves(dve, j // 8, j // 4 % 2)
                elif j == 8:
                    choice.pairs(dve, 0)
                elif j in (9, 10):
                    choice.sub_keys(dve, j - 9)
            mix.dve(dve, beats.get(HP, 0))
            choice.pairs(dve, 1)
            for o in range(2):
                mix.dve(dve, beats.get(HP + 1 + o, 0))
                choice.sub_keys(dve, o)
            choice.rows(dve, 1)
            mix.dve(dve, beats.get(HP + 3, 0))


def choose(nc, cst, scores, idx, gates, mix, tt, beats):
    with ExitStack() as ctx:
        t = Tools(nc, ctx)
        choice = Choice(t, cst, scores, idx, gates, tt)
        upto = lambda a, b: sum(beats.get(k, 0) for k in range(a, b))
        block = ctx.enter_context(nc.Block())

        @block.gpsimd
        def _(pool):
            mix.pool(pool, upto(0, 10))

        @block.tensor
        def _(pe):
            mix.pe(pe, mix.leftover(2) + upto(0, 10))

        @block.scalar
        def _(act):
            mix.act(act, mix.leftover(1))
            for g, (a, b) in enumerate(((0, 3), (3, 8))):
                mix.act(act, upto(a, b))
                choice.exps(act, g)
            mix.act(act, upto(8, 10))

        @block.vector
        def _(dve):
            choice.start(dve)
            for g in range(2):
                for part in range(2):
                    choice.halves(dve, g, part)
                    mix.dve(dve, beats.get(5 * g + part, 0))
                choice.pairs(dve, g)
                mix.dve(dve, beats.get(5 * g + 2, 0))
                choice.sub_keys(dve, 0)
                mix.dve(dve, beats.get(5 * g + 3, 0))
                choice.sub_keys(dve, 1)
                choice.rows(dve, g)
                mix.dve(dve, beats.get(5 * g + 4, 0))


def mix_rest(nc, dram, cst, mix, xn, h1, idx, gates, acc, out):
    with ExitStack() as ctx:
        t = Tools(nc, ctx)
        ident, done = cst["ident"], mix.at["pe"]
        assert done % BIG == 0 and set(mix.at.values()) == {done}
        stage = t.sb("stage", [P, 2, BIG], I32)
        uring, vring = t.sb("big_uring", [P, BIG, D]), t.sb("big_vring", [P, BIG, D])
        dots, acts, weights = (t.sb("big_" + n, [P, BIG]) for n in ("dots", "acts", "weights"))
        diag = t.sb("big_diag", [P, BIG, P])
        u_full = [t.sem(f"big_u_full{i}") for i in range(BIG)]
        v_full = [t.sem(f"big_v_full{i}") for i in range(BIG)]
        staged, issued, dotted, gelued = t.sem("staged"), t.sem("issued"), t.sem("big_dotted"), t.sem("big_gelued")
        weighted, diag_s, combined = t.sem("weighted"), t.sem("big_diag_s"), t.sem("big_combined")
        rows_out, stored = mix.rows_out, mix.stored
        first, last = done // BIG, XT * SLOTS // BIG
        per = SLOTS // BIG
        spans = [(max(first, tt * per), (tt + 1) * per, tt) for tt in range(XT) if (tt + 1) * per > first]
        block = ctx.enter_context(nc.Block())

        @block.sync
        def _(sp):
            for tt in range(XT):
                sp.wait_ge(rows_out, tt + 1)
                sp.dma_start(out[0, tt * P:(tt + 1) * P, :], h1[:, tt, :]).then_inc(stored, 16)
            sp.wait_ge(stored, 16 * XT)

        @block.gpsimd
        def _(pool):
            def group(count, at, hf):
                pool.tensor_copy(stage[:, hf, :], idx[:, at]).then_inc(staged, 1)
                pool.wait_ge(staged, count + 1)
                for k in range(BIG):
                    row = bass.IndirectOffsetOnAxis(ap=stage[:, hf, k:k + 1].bitcast(U32), axis=0)
                    pool.wait_ge(dotted, count * BIG + (k + 1))
                    pool.sem_inc(issued, 1)
                    pool.indirect_dma_start(uring[:, k, :], None, dram["expert_u"], row).then_inc(u_full[k], 16)
                    pool.wait_ge(combined, count * BIG + (k + 1))
                    pool.sem_inc(issued, 1)
                    pool.indirect_dma_start(vring[:, k, :], None, dram["expert_v"], row).then_inc(v_full[k], 16)

            pairs = (last - first) // 2
            with pool.Fori(0, pairs) as i:
                for hf in range(2):
                    group(i * 2 + hf, bass.ds(i * (2 * BIG) + (done + hf * BIG), BIG), hf)
            if (last - first) % 2:
                group(2 * pairs, slice(done + 2 * pairs * BIG, done + (2 * pairs + 1) * BIG), 0)

        @block.vector
        def _(dve):
            dve.sem_inc(dotted, BIG)
            if done % SLOTS == 0:
                mix.finish_tile(dve, done // SLOTS - 1)
            for a, b, tt in spans:
                with dve.Fori(a - first, b - first) as g:
                    for k in range(BIG):
                        dve.wait_ge(u_full[k], (g + 1) * 16)
                        dve.tensor_tensor_reduce(out=uring[:, k, :], in0=uring[:, k, :], in1=xn[:, tt, :], scale=1.0,
                                                 scalar=0.0, op0=ALU.mult, op1=ALU.add,
                                                 accum_out=dots[:, k:k + 1]).then_inc(dotted, 1)
                        if k % BIGHALF == BIGHALF - 1:
                            c = k + 1 - BIGHALF
                            dve.wait_ge(gelued, g * 2 + (k // BIGHALF + 1))
                            dve.tensor_tensor(weights[:, c:c + BIGHALF], acts[:, c:c + BIGHALF],
                                              gates[:, bass.ds(g * BIG + (done + c), BIGHALF)], ALU.mult
                                              ).then_inc(weighted, 1)
                dve.wait_ge(combined, BIG + BIG * (b - first))
                dve.tensor_copy(h1[:, tt, :], acc[:]).then_inc(rows_out, 1)

        @block.scalar
        def _(act):
            with act.Fori(0, last - first) as g:
                for hf in range(BIG // BIGHALF):
                    b = hf * BIGHALF
                    act.wait_ge(dotted, g * BIG + (b + BIGHALF + BIG))
                    act.activation(acts[:, b:b + BIGHALF], dots[:, b:b + BIGHALF], ACT.Gelu).then_inc(gelued, 1)
                    act.wait_ge(weighted, g * 2 + (hf + 1))
                    act.wait_ge(combined, g * BIG + (b + BIGHALF))
                    for k in range(b, b + BIGHALF):
                        act.activation(diag[:, k, :], ident[:], ACT.Copy, scale=weights[:, k:k + 1]).then_inc(diag_s, 1)

        @block.tensor
        def _(pe):
            pe.sem_inc(combined, BIG)
            for a, b, tt in spans:
                if a == tt * per:
                    mix.seed(pe, tt)
                with pe.Fori(a - first, b - first) as g:
                    for k in range(BIG):
                        pe.wait_ge(v_full[k], (g + 1) * 16)
                        pe.wait_ge(diag_s, g * BIG + (k + 1))
                        for n in range(2):
                            mm = pe.matmul(acc[:, n * 512:(n + 1) * 512], diag[:, k, :],
                                           vring[:, k, n * 512:(n + 1) * 512],
                                           start=False, stop=False, skip_group_check=True)
                        mm.then_inc(combined, 1)


def constants():
    i = np.arange(P)
    a, b = i[:, None], i[None, :]
    levels = np.zeros((P, LEVELS, P), np.float32)
    for l in range(LEVELS):
        s = 1 << l
        levels[:, l, :] = (a // (2 * s) == b // (2 * s)) & (a % (2 * s) < s) & (b % (2 * s) >= s)
    half = ROPE // 2
    inv = np.exp((-np.log(10000.0) * np.arange(half, dtype=np.float32) * np.float32(2.0 / ROPE)).astype(np.float32))
    ang = np.arange(T, dtype=np.float32)[:, None] * inv[None, :].astype(np.float32)

    halves = (i[:, None, None] // DK + 2 * np.arange(8)[None, :, None] == np.arange(16)[None, None, :]).astype(np.float32)

    def by_tile(x):
        out = np.zeros((P, NT, half), np.float32)
        for j in range(NT):
            out[0:SIZE[j], j] = x[START[j]:START[j] + SIZE[j]]
        return out
    return {
        "ident": np.eye(P, dtype=np.float32),
        "triu": (a <= b).astype(np.float32),
        "maskT": np.where(a <= b, 0.0, NEG).astype(np.float32),
        "mask": np.where(a >= b, 0.0, NEG).astype(np.float32),
        "levels": levels,
        "norm_sum": halves,
        "norm_spread": np.ascontiguousarray(halves.transpose(2, 1, 0)),
        "cos": by_tile(np.cos(ang).astype(np.float32)),
        "sin": by_tile(np.sin(ang).astype(np.float32)),
        "iota16": np.tile(np.arange(TOPK, dtype=np.float32), (P, 1)),
    }


def spread(keys, n):
    out, given = {}, 0
    for i, k in enumerate(keys):
        out[k] = (n * (i + 1) // len(keys)) // PAIR * PAIR - given
        given += out[k]
    return out


def layer(nc, dram, out, shapes):
    with ExitStack() as ctx:
        t = Tools(nc, ctx)
        cst = {name: t.sb("k_" + name, list(shape)) for name, shape in shapes.items()
               if name != "norm_spread"}
        cst["eps"] = t.sb("k_eps", [P, 1])
        cst["loaded"], cst["ident_loaded"], cst["eps_set"] = t.sem("consts_loaded"), t.sem("ident_loaded"), t.sem("eps_set")
        y, h1 = t.sb("y", [P, XT, D]), t.sb("h1", [P, XT, D])
        idx, gates = t.sb("idx", [P, XT * SLOTS], I32), t.sb("gates", [P, XT * SLOTS])
        acc = t.ps("acc", [P, D])
        with ExitStack() as front:
            f = Tools(nc, front)
            W = Weights(f, dram)
            mix = Mixing(nc, t, f, dram, cst, y, h1, idx, gates, acc, out, sum(SHARE.values()) + SHARE["choose"])
            state = {"hist": f.sb("hist", [P, QC, CONV - 1]), "cw": f.sb("conv_cols", [P, QC * CONV]),
                     "S": f.sb("S", [P, 4, DK]), "kT": f.sb("kT", [QKD, H, T]), "V": f.sb("V", [P, NT, H, 64]), "y": y}
            for part in range(len(PARTS)):
                NJ = len(PARTS[part])
                n = SHARE if part else dict.fromkeys(SHARE, 0)
                with ExitStack() as tokens:
                    m = Tools(nc, tokens)
                    keep = dict(state, rest=m.sb("rest", [P, NJ, REST]))
                    with ExitStack() as conv:
                        TP = sum(SIZE[j] for j in PARTS[part])
                        keep["sT"] = Tools(nc, conv).sb("sT", [P, QC, TP])
                        project(nc, dram, cst, keep, W, mix, part, spread(list(range(QC + 8)), n["project"]))
                        steps = [("n", c) for c in range(8)] if part else []
                        for jj in range(NJ):
                            steps += [("f", jj), ("g", jj), ("a", jj)] + [("l", jj, l) for l in range(1, LEVELS)] + [(k, jj) for k in "wvo"]
                        delta_rule(nc, dram, cst, keep, mix, part, spread(steps, n["delta_rule"]))
                    steps = [(k, jj) for jj in range(NJ) for k in "prt"] + [("u", i) for i in range(2 * H)]
                    latent_attention(nc, dram, cst, keep, mix, part, spread(steps, n["attention"]))
                out_project(nc, dram, cst, y, h1, W, mix, part, spread(list(range(8)), n["out_project"]))
                with ExitStack() as sel:
                    scores = Tools(nc, sel).sb("scores", [P, 2, 2 * H, KEYS])
                    own = part == 0
                    steps, k = (range(13, 2 * H + 4), "score_own") if own else (range(2 * H + 4), "score_and_choose")
                    score_and_choose(nc, dram, cst, y, scores, idx, gates, W, mix, part, spread(list(steps), SHARE[k]), own)
                    choose(nc, cst, scores, idx, gates, mix, 2 * part + 1, spread(list(range(10)), SHARE["choose"]))
        mix_rest(nc, dram, cst, mix, y, h1, idx, gates, acc, out)


_PLAIN = ["w_in", "conv_w", "w_uq", "w_ukv", "w_out", "w_pq", "expert_u", "expert_v"]
_VECTORS = ["attn_norm", "a_log", "dt_bias", "gdn_norm", "q_a_norm", "kv_a_norm", "q_norm", "k_norm", "ffn_norm"]


def kernel(**inputs):
    import numpy as _np
    import concourse.bacc as _bacc
    from concourse import mybir as _mybir
    from concourse.bass_utils import run_bass_kernel_spmd as _run

    arrays = {"x": inputs["x"][0], "meta": inputs["meta_tokens"], "sub_keys": inputs["sub_keys"][0]}
    for name in _PLAIN + _VECTORS:
        arrays[name] = inputs[name][0]
    consts = constants()
    for name, a in consts.items():
        arrays["c_" + name] = a
    arrays = {name: _np.ascontiguousarray(a) for name, a in arrays.items()}
    nc = _bacc.Bacc("TRN2", target_bir_lowering=False, num_devices=1)
    dram = {name: nc.dram_tensor(f"in_{name}", a.shape, _mybir.dt.from_np(a.dtype), kind="ExternalInput").ap()
            for name, a in arrays.items()}
    out = nc.dram_tensor("out_0", (1, SEQ, D), _mybir.dt.float32, kind="ExternalOutput").ap()
    layer(nc, dram, out, {name: a.shape for name, a in consts.items()})
    r = _run(nc, [{f"in_{name}": a for name, a in arrays.items()}], core_ids=[0])
    return r.results[0]["out_0"]
```
